# Optimizing a Trainium2 kernel written in Bass

```python
import math
import jax, jax.numpy as jnp
from jax import lax
import numpy as np

D_MODEL = 1024
BATCH = 1
SEQ = 512
DEPTH = 1

DIFF_HEADS = 4
DIFF_HD = 64
DIFF_VD = 2 * DIFF_HD
DIFF_W = DIFF_HEADS * DIFF_VD
NSA_HEADS = 8
NSA_KV = 2
NSA_GQ = NSA_HEADS // NSA_KV
NSA_HD = 64
NSA_W = NSA_HEADS * NSA_HD
MIX_W = DIFF_W + NSA_W
CMP_LEN = 32
CMP_STRIDE = 16
CMP_HIDDEN = 256
SLC_BLOCK = 64
SLC_TOPK = 16
WINDOW = 512
Q_BLOCK = 128
SLC_Q_CHUNK = 64
N_BUCKETS = 32
MAX_DISTANCE = 128
N_BIAS_HEADS = DIFF_HEADS + NSA_HEADS
D_FF = -(-8 * D_MODEL // (3 * 256)) * 256
NSA_KV_W = NSA_KV * NSA_HD
N_IN = 3 * DIFF_HEADS * 2 * DIFF_HD + NSA_W + 6 * NSA_KV_W + 3 * NSA_HEADS
NEG = -1e30
EPS = 1e-6

kernel_name = "hymba_diff_nsa_block"

def rms_norm(x, g):
    xf = x.astype(jnp.float32)
    y = xf * lax.rsqrt(jnp.mean(xf * xf, axis=-1, keepdims=True) + EPS)
    return (y * g.astype(jnp.float32)).astype(x.dtype)

def t5_bucket(dist):
    dist = jnp.maximum(dist, 0)
    max_exact = N_BUCKETS // 2
    large = max_exact + (jnp.log(jnp.maximum(dist, 1).astype(jnp.float32) / max_exact)
                         / math.log(MAX_DISTANCE / max_exact) * (N_BUCKETS - max_exact)).astype(jnp.int32)
    large = jnp.minimum(large, N_BUCKETS - 1)
    return jnp.where(dist < max_exact, dist, large)

def diff_attention(q, k, v, lam, subln_g, lambda_init, bias_tab):
    B, H, _, T, d = q.shape
    nb = T // Q_BLOCK
    scale = d ** -0.5
    q_b = q.reshape(B, H, 2, nb, Q_BLOCK, d).transpose(3, 0, 1, 2, 4, 5)
    kpos = jnp.arange(T)

    def block(args):
        q_blk, i = args
        qpos = i * Q_BLOCK + jnp.arange(Q_BLOCK)
        dist = qpos[:, None] - kpos[None, :]
        bias = bias_tab[t5_bucket(dist)].astype(jnp.float32).transpose(2, 0, 1)
        s = jnp.einsum('bhiqd,bhikd->bhiqk', q_blk, k).astype(jnp.float32) * scale + bias[None, :, None]
        p = jax.nn.softmax(jnp.where((dist >= 0)[None, None, None], s, NEG), axis=-1)
        a = p[:, :, 0] - lam * p[:, :, 1]
        return jnp.einsum('bhqk,bhkv->bhqv', a.astype(v.dtype), v)

    o = lax.map(block, (q_b, jnp.arange(nb)))
    o = o.transpose(1, 2, 0, 3, 4).reshape(B, H, T, -1)
    o = rms_norm(o, subln_g) * (1.0 - lambda_init)
    return o.transpose(0, 2, 1, 3).reshape(B, T, -1)

def nsa_attention(q, k_c, v_c, k_s, v_s, k_w, v_w, gates,
                  pos_k, w1_k, w2_k, pos_v, w1_v, w2_v, bias_nsa):
    B, G, Hg, T, d = q.shape
    dt = q.dtype
    scale = d ** -0.5
    tpos = jnp.arange(T)

    n_cmp = (T - CMP_LEN) // CMP_STRIDE + 1
    cmp_start = jnp.arange(n_cmp) * CMP_STRIDE
    cmp_end = cmp_start + CMP_LEN - 1
    win = cmp_start[:, None] + jnp.arange(CMP_LEN)[None, :]

    def compress(kk, pos, w1, w2):
        blocks = (kk[:, :, win] + pos).reshape(B, G, n_cmp, CMP_LEN * d)
        return jax.nn.gelu(blocks @ w1) @ w2

    kc = compress(k_c, pos_k, w1_k, w2_k)
    vc = compress(v_c, pos_v, w1_v, w2_v)
    cmask = cmp_end[None, :] <= tpos[:, None]
    has_cmp = (tpos >= CMP_LEN - 1).astype(jnp.float32)
    s = jnp.einsum('bgqtd,bgnd->bgqtn', q, kc).astype(jnp.float32) * scale
    p_cmp = jax.nn.softmax(jnp.where(cmask, s, NEG), axis=-1) * has_cmp[:, None]
    o_cmp = jnp.einsum('bgqtn,bgnd->bgqtd', p_cmp.astype(dt), vc)

    n_slc = T // SLC_BLOCK
    slc_start = jnp.arange(n_slc) * SLC_BLOCK
    overlap = ((cmp_start[:, None] < slc_start[None, :] + SLC_BLOCK)
               & (cmp_end[:, None] >= slc_start[None, :])).astype(jnp.float32)
    imp = jnp.einsum('bgqtn,nj->bgtj', p_cmp, overlap)
    cur = tpos // SLC_BLOCK
    j = jnp.arange(n_slc)
    valid = slc_start[None, :] <= tpos[:, None]
    forced = (j[None, :] == 0) | (j[None, :] == cur[:, None]) | (j[None, :] == cur[:, None] - 1)
    imp = jnp.where(forced, jnp.inf, jnp.where(valid, imp, -jnp.inf))
    k_top = min(SLC_TOPK, n_slc)
    _, sel = lax.top_k(imp, k_top)

    ks_blk = k_s.reshape(B, G, n_slc, SLC_BLOCK, d)
    vs_blk = v_s.reshape(B, G, n_slc, SLC_BLOCK, d)
    bias_g = bias_nsa.transpose(1, 0, 2)
    nc = T // SLC_Q_CHUNK
    q_ch = q.reshape(B, G, Hg, nc, SLC_Q_CHUNK, d).transpose(3, 0, 1, 2, 4, 5)
    sel_ch = sel.reshape(B, G, nc, SLC_Q_CHUNK, k_top).transpose(2, 0, 1, 3, 4)
    bi = jnp.arange(B)[:, None, None, None]
    gi = jnp.arange(G)[None, :, None, None]
    gi5 = jnp.arange(G)[None, :, None, None, None]

    def slc_chunk(args):
        q_c, sel_c, ci = args
        qpos = ci * SLC_Q_CHUNK + jnp.arange(SLC_Q_CHUNK)
        kg = ks_blk[bi, gi, sel_c]
        vg = vs_blk[bi, gi, sel_c]
        kpos = sel_c[..., None] * SLC_BLOCK + jnp.arange(SLC_BLOCK)
        dist = qpos[None, None, :, None, None] - kpos
        bias = bias_g[gi5, t5_bucket(dist)].astype(jnp.float32).transpose(0, 1, 5, 2, 3, 4)
        sc = jnp.einsum('bgqcd,bgckld->bgqckl', q_c, kg).astype(jnp.float32) * scale + bias
        sc = jnp.where((dist >= 0)[:, :, None], sc, NEG).reshape(B, G, Hg, SLC_Q_CHUNK, -1)
        p = jax.nn.softmax(sc, axis=-1).reshape(B, G, Hg, SLC_Q_CHUNK, k_top, SLC_BLOCK)
        return jnp.einsum('bgqckl,bgckld->bgqcd', p.astype(dt), vg)

    o_slc = lax.map(slc_chunk, (q_ch, sel_ch, jnp.arange(nc)))
    o_slc = o_slc.transpose(1, 2, 3, 0, 4, 5).reshape(B, G, Hg, T, d)

    k_pad = jnp.pad(k_w, ((0, 0), (0, 0), (WINDOW, 0), (0, 0)))
    v_pad = jnp.pad(v_w, ((0, 0), (0, 0), (WINDOW, 0), (0, 0)))
    nb = T // Q_BLOCK
    q_b = q.reshape(B, G, Hg, nb, Q_BLOCK, d).transpose(3, 0, 1, 2, 4, 5)

    def win_block(args):
        q_blk, i = args
        start = i * Q_BLOCK
        kb = lax.dynamic_slice_in_dim(k_pad, start, WINDOW + Q_BLOCK, axis=2)
        vb = lax.dynamic_slice_in_dim(v_pad, start, WINDOW + Q_BLOCK, axis=2)
        qpos = start + jnp.arange(Q_BLOCK)
        kpos = start - WINDOW + jnp.arange(WINDOW + Q_BLOCK)
        dist = qpos[:, None] - kpos[None, :]
        mask = (dist >= 0) & (dist < WINDOW) & (kpos[None, :] >= 0)
        bias = bias_nsa[t5_bucket(dist)].astype(jnp.float32).transpose(2, 3, 0, 1)
        sc = jnp.einsum('bgqtd,bgsd->bgqts', q_blk, kb).astype(jnp.float32) * scale + bias
        p = jax.nn.softmax(jnp.where(mask, sc, NEG), axis=-1)
        return jnp.einsum('bgqts,bgsd->bgqtd', p.astype(dt), vb)

    o_win = lax.map(win_block, (q_b, jnp.arange(nb)))
    o_win = o_win.transpose(1, 2, 3, 0, 4, 5).reshape(B, G, Hg, T, d)

    o = gates[..., 0:1] * o_cmp + gates[..., 1:2] * o_slc + gates[..., 2:3] * o_win
    return o.transpose(0, 3, 1, 2, 4).reshape(B, T, G * Hg * d)

def setup_inputs(seed: int = 0) -> dict:
    key = jax.random.key(seed)
    ks = jax.random.split(key, 24)
    f32 = jnp.float32
    nrm = lambda k, shape, s: (jax.random.normal(k, shape, f32) * s)
    gain = lambda k, shape: 1.0 + 0.05 * jax.random.normal(k, shape, f32)
    L = DEPTH
    return {
        "x": jax.random.normal(ks[0], (BATCH, SEQ, D_MODEL), f32),
        "norm1": gain(ks[1], (L, D_MODEL)),
        "w_in": nrm(ks[2], (L, D_MODEL, N_IN), D_MODEL ** -0.5),
        "lambda_q1": nrm(ks[3], (L, DIFF_HD), 0.1),
        "lambda_k1": nrm(ks[4], (L, DIFF_HD), 0.1),
        "lambda_q2": nrm(ks[5], (L, DIFF_HD), 0.1),
        "lambda_k2": nrm(ks[6], (L, DIFF_HD), 0.1),
        "diff_subln": gain(ks[7], (L, DIFF_VD)),
        "cmp_pos_k": nrm(ks[8], (L, CMP_LEN, NSA_HD), 0.5),
        "cmp_w1_k": nrm(ks[9], (L, CMP_LEN * NSA_HD, CMP_HIDDEN), (CMP_LEN * NSA_HD) ** -0.5),
        "cmp_w2_k": nrm(ks[10], (L, CMP_HIDDEN, NSA_HD), CMP_HIDDEN ** -0.5),
        "cmp_pos_v": nrm(ks[11], (L, CMP_LEN, NSA_HD), 0.5),
        "cmp_w1_v": nrm(ks[12], (L, CMP_LEN * NSA_HD, CMP_HIDDEN), (CMP_LEN * NSA_HD) ** -0.5),
        "cmp_w2_v": nrm(ks[13], (L, CMP_HIDDEN, NSA_HD), CMP_HIDDEN ** -0.5),
        "nsa_norm": gain(ks[14], (L, NSA_W)),
        "w_out": nrm(ks[15], (L, MIX_W, D_MODEL), MIX_W ** -0.5),
        "norm2": gain(ks[16], (L, D_MODEL)),
        "w_gate": nrm(ks[17], (L, D_MODEL, D_FF), D_MODEL ** -0.5),
        "w_up": nrm(ks[18], (L, D_MODEL, D_FF), D_MODEL ** -0.5),
        "w_down": nrm(ks[19], (L, D_FF, D_MODEL), D_FF ** -0.5),
        "rel_bias": nrm(ks[20], (N_BUCKETS, N_BIAS_HEADS), 0.5),
        "final_norm": gain(ks[21], (D_MODEL,)),
    }

def reference(x, norm1, w_in, lambda_q1, lambda_k1, lambda_q2, lambda_k2, diff_subln,
              cmp_pos_k, cmp_w1_k, cmp_w2_k, cmp_pos_v, cmp_w1_v, cmp_w2_v, nsa_norm,
              w_out, norm2, w_gate, w_up, w_down, rel_bias, final_norm):
    B, T, _ = x.shape
    G, Hg, d = NSA_KV, NSA_GQ, NSA_HD
    bias_diff = rel_bias[:, :DIFF_HEADS]
    bias_nsa = rel_bias[:, DIFF_HEADS:].reshape(N_BUCKETS, G, Hg)
    qk_w = DIFF_HEADS * 2 * DIFF_HD
    splits = np.cumsum([qk_w, qk_w, DIFF_W, NSA_W] + [NSA_KV_W] * 6).tolist()
    for l in range(DEPTH):
        lambda_init = 0.8 - 0.6 * math.exp(-0.3 * l)
        h = rms_norm(x, norm1[l])
        proj = h @ w_in[l]
        (dq, dk, dv, nq, kc, vc, ksl, vsl, kw, vw, gt) = jnp.split(proj, splits, axis=-1)

        dq = dq.reshape(B, T, DIFF_HEADS, 2, DIFF_HD).transpose(0, 2, 3, 1, 4)
        dk = dk.reshape(B, T, DIFF_HEADS, 2, DIFF_HD).transpose(0, 2, 3, 1, 4)
        dv = dv.reshape(B, T, DIFF_HEADS, DIFF_VD).transpose(0, 2, 1, 3)
        lam = (jnp.exp(jnp.sum(lambda_q1[l].astype(jnp.float32) * lambda_k1[l].astype(jnp.float32)))
               - jnp.exp(jnp.sum(lambda_q2[l].astype(jnp.float32) * lambda_k2[l].astype(jnp.float32)))
               + lambda_init)
        o_diff = diff_attention(dq, dk, dv, lam, diff_subln[l], lambda_init, bias_diff)

        to_kv = lambda a: a.reshape(B, T, G, d).transpose(0, 2, 1, 3)
        nq = nq.reshape(B, T, G, Hg, d).transpose(0, 2, 3, 1, 4)
        gates = jax.nn.sigmoid(gt.reshape(B, T, G, Hg, 3).transpose(0, 2, 3, 1, 4))
        o_nsa = nsa_attention(nq, to_kv(kc), to_kv(vc), to_kv(ksl), to_kv(vsl), to_kv(kw), to_kv(vw),
                              gates, cmp_pos_k[l], cmp_w1_k[l], cmp_w2_k[l],
                              cmp_pos_v[l], cmp_w1_v[l], cmp_w2_v[l], bias_nsa)
        o_nsa = rms_norm(o_nsa, nsa_norm[l])

        x = x + jnp.concatenate([o_diff, o_nsa], axis=-1) @ w_out[l]
        h = rms_norm(x, norm2[l])
        x = x + (jax.nn.silu(h @ w_gate[l]) * (h @ w_up[l])) @ w_down[l]
    return rms_norm(x, final_norm)


_drawn_inputs = setup_inputs


def setup_inputs(seed=0):
    import zlib

    import numpy as np

    out = dict(_drawn_inputs(seed))
    spreads = {}
    factors = {'lambda_q1': 4.361, 'lambda_k1': 3.167, 'lambda_q2': 8.0}
    for name, (base, spread) in spreads.items():
        noise = np.random.default_rng([zlib.crc32(name.encode()), seed]).standard_normal(out[name].shape)
        drawn = base * np.exp(spread * noise) if base else spread * noise
        out[name] = __import__('jax').numpy.asarray(drawn.astype(out[name].dtype))
    for name, factor in factors.items():
        out[name] = (out[name] * factor).astype(out[name].dtype)
    return out
```

```python
import math
from contextlib import ExitStack

import numpy as np

import concourse.bass as bass
from concourse import mybir

F32 = mybir.dt.float32
F32R = mybir.dt.float32r
ALU = mybir.AluOpType
ACT = mybir.ActivationFunctionType
AX = mybir.AxisListType

P = 128
D = 1024
T = 512
NT = T // P
KT = D // P
DIFF_HEADS, HD = 4, 64
NSA_HEADS, GROUPS = 8, 2
HEADS_PER_GROUP = NSA_HEADS // GROUPS
NHEADS = DIFF_HEADS + NSA_HEADS
N_BUCKETS, MAX_DISTANCE = 32, 128
CMP_LEN, CMP_STRIDE, CMP_HIDDEN = 32, 16, 256
N_CMP = (T - CMP_LEN) // CMP_STRIDE + 1
NC = 32
D_FF = 2816
FT = D_FF // P
EPS = 1e-6
NEG = 1e30
SCALE = HD ** -0.5
LAMBDA_INIT = 0.8 - 0.6 * math.exp(0.0)
COL = {"dq": 0, "dk": 512, "dv": 1024, "nq": 1536, "kc": 2048, "vc": 2176, "ksl": 2304, "vsl": 2432,
       "kw": 2560, "vw": 2688, "gt": 2816}
GATES = 24

RAW_SLOTS = 4
SPLIT_SLOTS = 4
E_SLOTS = 4
BIAS_SLOTS = 3
PIECES = 8
PIECES_PER_SLOT = 1.4


def shape_constants():
    ident = np.eye(P, dtype=np.float32)
    dist = 255 - np.arange(384)
    half = N_BUCKETS // 2
    pos = np.maximum(dist, 1).astype(np.float32)
    far = half + (np.log(pos / half) / math.log(MAX_DISTANCE / half) * (N_BUCKETS - half)).astype(np.int32)
    bucket = np.where(dist < half, np.maximum(dist, 0), np.minimum(far, N_BUCKETS - 1))
    choice = np.zeros((N_BUCKETS, 384), np.float32)
    for j in range(384):
        if dist[j] >= 0:
            choice[bucket[j], j] -= 1.0
            choice[N_BUCKETS - 1, j] += 1.0
    causal = np.broadcast_to(np.where(dist < 0, np.float32(NEG), np.float32(0)), (NHEADS, 384))
    q = np.arange(T)[:, None]
    n = np.arange(NC)[None, :]
    hidden = (n * CMP_STRIDE + CMP_LEN - 1 > q) | (n >= N_CMP)
    cmask = np.where(hidden, np.float32(NEG), np.float32(0)).reshape(NT, P, NC).transpose(1, 0, 2)
    has = (np.arange(T) >= CMP_LEN - 1).astype(np.float32).reshape(NT, P).T
    return {"c_ident": ident, "c_choice": choice, "c_causal": np.ascontiguousarray(causal),
            "c_cmask": np.ascontiguousarray(cmask), "c_has": np.ascontiguousarray(has)}


def plan_chunks():
    chunks = [("c", 0), ("c", 1), ("k", "ksl"), ("v", "vsl"), ("k", "kw"), ("v", "vw"), ("g", 0), ("q", 0)]
    base = len(chunks)
    for item in (1, "d0", 2, "d1", 3, "d2", "d3"):
        if isinstance(item, int):
            chunks.append(("q", item))
        else:
            h = int(item[1])
            chunks += [("dq", h), ("dk", h), ("dv", h)]
    proj = len(chunks)
    chunks += [("o", (dh, kc)) for dh in range(2) for kc in range(4)]
    for f in range(FT):
        chunks += [("gate", f), ("up", f)]
    chunks += [("down", (dh, kc)) for dh in range(2) for kc in range(FT // 2)]
    return chunks, base, proj


def plan_slots():
    slots = []

    def nsa(pair):
        for h in (2 * pair, 2 * pair + 1):
            for b in range(2):
                slots.extend(("nsa", h, b, i) for i in range(NT))

    def diff(h):
        slots.extend(("diff", h, m, i) for i in range(NT) for m in range(2))

    nsa(0), nsa(1), diff(0), nsa(2), diff(1), nsa(3)
    slots.extend(("cmp", 0, 0, t) for t in range(NT))
    diff(2), diff(3)
    return slots


def hymba_block(nc, x, norm1, w_in, lambda_q1, lambda_k1, lambda_q2, lambda_k2, diff_subln,
                cmp_pos_k, cmp_w1_k, cmp_w2_k, cmp_pos_v, cmp_w1_v, cmp_w2_v, nsa_norm,
                w_out, norm2, w_gate, w_up, w_down, rel_bias, final_norm,
                c_ident, c_choice, c_causal, c_cmask, c_has, bias_scratch, bias_rows, out):
    chunks, n_base, n_proj = plan_chunks()
    slots = plan_slots()
    n_slots = len(slots)
    index = {c: k for k, c in enumerate(chunks)}
    n_out0, n_ffn0 = index[("o", (0, 0))], index[("gate", 0)]
    n_down0 = index[("down", (0, 0))]

    raws = []
    for k, c in enumerate(chunks):
        raws.append(("chunk", k))
        if c == ("k", "ksl"):
            raws += [("w1", (0, m, j)) for m in range(2) for j in range(2)]
        if c == ("v", "vsl"):
            raws += [("w1", (1, m, j)) for m in range(2) for j in range(2)]
    raw_of = {r: n for n, r in enumerate(raws)}
    w1_order = [r[1] for r in raws if r[0] == "w1"]

    def needed(slot):
        kind, h, _, _ = slot
        if kind == "diff":
            return index[("dv", h)] + 1
        return index[("q", 3 if kind == "cmp" else h // 2)] + 1

    n_pieces = (n_proj - n_base) * PIECES
    piece_upto, done = [], 0
    for s in range(n_slots):
        ahead = min(s + 1, n_slots - 1)
        done = max(done, min(n_pieces, int(PIECES_PER_SLOT * (s + 1))), (needed(slots[ahead]) - n_base) * PIECES)
        piece_upto.append(done)
    chunks_done_in = [[] for _ in range(n_slots)]
    for k in range(n_base, n_proj):
        s = next(s for s in range(n_slots) if piece_upto[s] >= (k - n_base + 1) * PIECES)
        chunks_done_in[s].append(k)

    turned = [s for s in range(n_slots) if not (slots[s][0] == "diff" and slots[s][2] == 0)]
    turn = {s: n for n, s in enumerate(turned)}
    turns_upto = [sum(1 for x_ in turned if x_ <= s) for s in range(n_slots)]

    def bias_head(slot):
        return slot[1] if slot[0] == "diff" else DIFF_HEADS + slot[1]

    bias_order = []
    for s in slots:
        if s[0] != "cmp" and bias_head(s) not in bias_order:
            bias_order.append(bias_head(s))
    bias_first = {h: min(i for i, s in enumerate(slots) if s[0] != "cmp" and bias_head(s) == h) for h in bias_order}
    bias_last = {h: max(i for i, s in enumerate(slots) if s[0] != "cmp" and bias_head(s) == h) for h in bias_order}
    last_diff_qk = {h: max(i for i, s in enumerate(slots) if s[0] == "diff" and s[1] == h) for h in range(DIFF_HEADS)}

    hi_upto, n_hi = [], 0
    for c in chunks[:n_proj]:
        if c[0] in ("q", "k", "dq", "dk"):
            n_hi += 2
        hi_upto.append(n_hi)

    with ExitStack() as ctx:
        def sem(name):
            return ctx.enter_context(nc.semaphore(name))

        def sb(name, shape, dt=F32, stack=ctx):
            return stack.enter_context(nc.sbuf_tensor(name, shape, dt))

        ps = [ctx.enter_context(nc.psum_tensor(f"bank{b}", [P, 512], F32)) for b in range(8)]
        PROJ, SCORE, TURN, OUTP = ps[0:2], ps[2:4], ps[4:6], ps[6:8]
        FOUR = [[ps[0], ps[1], ps[6], ps[7]], [ps[2], ps[3], ps[4], ps[5]]]

        ident = sb("ident", [P, P])
        rows = sb("rows", [P, P])
        cols = sb("cols", [P, 56])
        relb = sb("relb", [N_BUCKETS, NHEADS])
        cmask = sb("cmask", [P, NT, NC])
        has_cmp = sb("has_cmp", [P, NT])
        lam = sb("lam", [P, 8])
        w2 = sb("w2", [P, 2, 2, HD])
        stat = sb("stat", [P, 64])
        gates = sb("gates", [P, NT, GATES])
        nmax = sb("nmax", [P, n_slots])
        ssum = sb("ssum", [P, n_slots])
        coef = sb("coef", [P, n_slots])
        cstat = sb("cstat", [P, NT, 4, NSA_HEADS])
        sq = sb("sq", [P, 512])
        xres = sb("xres", [P, NT, D])
        xT_hi = sb("xT_hi", [P, KT, T], F32R)
        xT_lo = sb("xT_lo", [P, KT, T], F32R)
        raw = sb("raw", [P, RAW_SLOTS, 1024])
        w_hi = sb("w_hi", [P, SPLIT_SLOTS, 1024], F32R)
        w_lo = sb("w_lo", [P, SPLIT_SLOTS, 1024], F32R)

        with ExitStack() as attention:
            mix = sb("mix", [P, NT, D], F32, attention)
            q_nsa = sb("q_nsa", [P, NSA_HEADS, T], F32R, attention)
            k_nsa = sb("k_nsa", [P, 2, 2 * GROUPS, T], F32R, attention)
            v_nsa = sb("v_nsa", [P, 2, NT, P], F32, attention)
            v_diff = sb("v_diff", [P, 2, NT, P], F32, attention)
            bias = sb("bias", [P, BIAS_SLOTS, 512], F32, attention)
            E = sb("E", [P, E_SLOTS, 512], F32, attention)
            PT = sb("PT", [P, 2, 512], F32, attention)
            kc_s = sb("kc_s", [P, 2, GROUPS, NC], F32R, attention)
            vc_bd = sb("vc_bd", [P, GROUPS, 4 * HD], F32, attention)
            hid = sb("hid", [P, 2, 2, GROUPS * NC], F32, attention)
            with ExitStack() as compress:
                blk = [sb(f"blk{i}", [P, 16, GROUPS, NC], F32, compress) for i in range(2)]
                choice = sb("choice", [N_BUCKETS, 384], F32, compress)
                causal = sb("causal", [NHEADS, 384], F32, compress)
                bias_vec = sb("bias_vec", [NHEADS, 384], F32, compress)
                lam_in = sb("lam_in", [P, 4, HD], F32, compress)
            q_diff = sb("q_diff", [P, 2, 2, T], F32R, attention)
            k_diff = sb("k_diff", [P, 2, 2, 2, T], F32R, attention)
        with ExitStack() as swiglu:
            act_hi = sb("act_hi", [P, FT, T], F32R, swiglu)
            act_lo = sb("act_lo", [P, FT, T], F32R, swiglu)
            silu_g = sb("silu_g", [P, 2, T], F32, swiglu)
            prod = sb("prod", [P, 2, T], F32, swiglu)
            final_g = sb("final_g", [P, D], F32, swiglu)

        s_x = [sem(f"s_x{t}") for t in range(NT)]
        s_ident, s_rows, s_btab, s_small, s_lamin = sem("s_ident"), sem("s_rows"), sem("s_btab"), sem("s_small"), sem("s_lamin")
        s_raw = [sem(f"s_raw{i}") for i in range(RAW_SLOTS)]
        s_bias = [sem(f"s_bias{i}") for i in range(BIAS_SLOTS)]
        s_scratch, s_spread = sem("s_scratch"), sem("s_spread")
        s_whi, s_split = sem("s_whi"), sem("s_split")
        s_chunk = sem("s_chunk")
        s_w1 = sem("s_w1")
        s_cols_t, s_cols = sem("s_cols_t"), sem("s_cols")
        s_bvec_p, s_bvec = sem("s_bvec_p"), sem("s_bvec")
        s_ss, s_root_in, s_root, s_norm = sem("s_ss"), sem("s_root_in"), sem("s_root"), sem("s_norm")
        s_tp, s_thi, s_tlo = sem("s_tp"), sem("s_thi"), sem("s_tlo")
        s_hi, s_evac = sem("s_hi"), sem("s_evac")
        s_gexp_in, s_gexp = sem("s_gexp_in"), sem("s_gexp")
        s_lamdot, s_lamexp = sem("s_lamdot"), sem("s_lamexp")
        s_hid, s_gelu = sem("s_hid"), sem("s_gelu")
        s_kvc, s_kchi, s_cmp_ready = sem("s_kvc"), sem("s_kchi"), sem("s_cmp_ready")
        s_zero = sem("s_zero")
        s_qk, s_add, s_exp, s_comb = sem("s_qk"), sem("s_add"), sem("s_exp"), sem("s_comb")
        s_turn, s_pt, s_pv, s_of = sem("s_turn"), sem("s_pt"), sem("s_pv"), sem("s_of")
        s_coefs, s_resid = sem("s_coefs"), sem("s_resid")
        s_silu, s_prod, s_ahi, s_alo = sem("s_silu"), sem("s_prod"), sem("s_ahi"), sem("s_alo")
        s_y, s_out = sem("s_y"), sem("s_out")
        s_dve = sem("s_dve")

        C_N1, C_N2, C_SUB, C_NSA, C_POS = 0, 8, 16, 17, 21
        N_ROWS = 53

        def wv_hi(k):
            return w_hi[:, k % SPLIT_SLOTS, :]

        def wv_lo(k):
            return w_lo[:, k % SPLIT_SLOTS, :]

        def chunk_src(k):
            kind, a = chunks[k]
            if kind in ("o", "down"):
                w = w_out if kind == "o" else w_down
                dh, kc = a
                return w[0].rearrange("(k p) n -> p k n", p=P)[:, 2 * kc:2 * kc + 2, 512 * dh:512 * dh + 512]
            if kind in ("gate", "up"):
                w, c0 = (w_gate if kind == "gate" else w_up), P * a
            elif kind == "c":
                w, c0 = w_in, COL["kc" if a == 0 else "vc"]
            elif kind in ("k", "v"):
                w, c0 = w_in, COL[a]
            elif kind == "g":
                w, c0 = w_in, COL["gt"]
            elif kind == "q":
                w, c0 = w_in, COL["nq"] + P * a
            else:
                w, c0 = w_in, COL[kind] + P * a
            n = GATES if kind == "g" else P
            return w[0].rearrange("(k p) n -> p k n", p=P)[:, :, c0:c0 + n]

        def chunk_cols(k):
            return KT * GATES if chunks[k][0] == "g" else 1024

        block = ctx.enter_context(nc.Block())

        @block.sync
        def _(sp):
            for t in range(NT):
                sp.dma_start(xres[:, t, :], x[0, t * P:(t + 1) * P, :]).then_inc(s_x[t], 16)
            for n, (what, a) in enumerate(raws):
                if n >= RAW_SLOTS:
                    was, b = raws[n - RAW_SLOTS]
                    if was == "chunk":
                        sp.wait_ge(s_split, b + 1)
                    else:
                        sp.wait_ge(s_w1, w1_order.index(b) + 1)
                dst = raw[:, n % RAW_SLOTS, :]
                if what == "chunk":
                    src = chunk_src(a)
                    dst = dst[:, 0:chunk_cols(a)].rearrange("p (k n) -> p k n", k=src.shape[1])
                else:
                    kv, m, j = a
                    w1 = (cmp_w1_k, cmp_w1_v)[kv]
                    src = w1[0].rearrange("(j p) n -> p j n", p=P)[:, 8 * j:8 * j + 8, P * m:P * m + P]
                    dst = dst.rearrange("p (k n) -> p k n", k=8)
                sp.dma_start(dst, src).then_inc(s_raw[n % RAW_SLOTS], 16)
            for t in range(NT):
                sp.wait_ge(s_y, t + 1)
                sp.dma_start(out[0, t * P:(t + 1) * P, :], xres[:, t, :]).then_inc(s_out, 16)
            sp.wait_ge(s_out, 16 * NT)

        def raw_landed(eng, item):
            n = raw_of[item]
            eng.wait_ge(s_raw[n % RAW_SLOTS], 16 * (n // RAW_SLOTS + 1))

        @block.gpsimd
        def _(pool):
            for k in range(len(chunks)):
                n = chunk_cols(k)
                src = raw[:, raw_of[("chunk", k)] % RAW_SLOTS, 0:n]
                raw_landed(pool, ("chunk", k))
                if k >= SPLIT_SLOTS:
                    pool.wait_ge(s_chunk, k - SPLIT_SLOTS + 1)
                nc.gpsimd.tensor_copy(wv_hi(k)[:, 0:n], src).then_inc(s_whi, 1)
                pool.wait_ge(s_whi, k + 1)
                nc.gpsimd.tensor_tensor(wv_lo(k)[:, 0:n], src, wv_hi(k)[:, 0:n].bitcast(F32),
                                        ALU.subtract).then_inc(s_split, 1)

        @block.tensor
        def _(pe):
            def three(o, a_hi, a_lo, b_hi, b_lo, first, last):
                nc.tensor.matmul(o, a_hi, b_hi, start=first, stop=False)
                nc.tensor.matmul(o, a_hi, b_lo, start=False, stop=False)
                return nc.tensor.matmul(o, a_lo, b_hi, start=False, stop=last)

            def turn_rows(stage, ready):
                ready()
                src = mix
                for kt in range(KT):
                    n = stage * KT + kt
                    if kt >= 4:
                        pe.wait_ge(s_tlo, n - 3)
                    bank = ps[2 + kt % 4]
                    for t in range(NT):
                        mm = nc.tensor.transpose(bank[:, t * P:(t + 1) * P], src[:, t, kt * P:(kt + 1) * P], ident[:, :])
                    mm.then_inc(s_tp, 1)

            def proj_piece(k, piece):
                kind = chunks[k][0]
                bank = PROJ[k % 2]
                if piece == 0:
                    pe.wait_ge(s_split, k + 1)
                    if k >= 2:
                        pe.wait_ge(s_evac, k - 1)
                if kind in ("v", "dv", "g"):
                    n = GATES if kind == "g" else P
                    hi = wv_hi(k)[:, 0:KT * n].rearrange("p (k n) -> p k n", k=KT)
                    lo = wv_lo(k)[:, 0:KT * n].rearrange("p (k n) -> p k n", k=KT)
                    t, half = piece // 2, piece % 2
                    for kt in range(4 * half, 4 * half + 4):
                        mm = three(bank[:, t * n:(t + 1) * n], xT_hi[:, kt, t * P:(t + 1) * P],
                                   xT_lo[:, kt, t * P:(t + 1) * P], hi[:, kt, :], lo[:, kt, :],
                                   kt == 0, kt == KT - 1)
                else:
                    kt = piece
                    hi, lo = wv_hi(k)[:, kt * P:(kt + 1) * P], wv_lo(k)[:, kt * P:(kt + 1) * P]
                    nc.tensor.matmul(bank[:, :], hi, xT_hi[:, kt, :], start=kt == 0, stop=False)
                    nc.tensor.matmul(bank[:, :], hi, xT_lo[:, kt, :], start=False, stop=False)
                    mm = nc.tensor.matmul(bank[:, :], lo, xT_hi[:, kt, :], start=False, stop=kt == KT - 1)
                if piece == PIECES - 1:
                    mm.then_inc(s_chunk, 1)

            def proj_chunk(k):
                for piece in range(PIECES):
                    proj_piece(k, piece)

            def hidden(kv):
                pe.wait_ge(s_evac, kv + 1)
                for m in range(2):
                    bank = ps[2 + 2 * kv + m]
                    for j in range(2):
                        raw_landed(pe, ("w1", (kv, m, j)))
                        w = raw[:, raw_of[("w1", (kv, m, j))] % RAW_SLOTS, :]
                        for jj in range(8):
                            mm = nc.tensor.matmul(bank[:, 0:GROUPS * NC], w[:, jj * P:(jj + 1) * P],
                                                  blk[kv][:, 8 * j + jj, :, :].rearrange("p g n -> p (g n)"),
                                                  start=(j == 0 and jj == 0), stop=(j == 1 and jj == 7))
                        mm.then_inc(s_w1, 1)

            def compressed():
                pe.wait_ge(s_small, 16 * 4)
                pe.wait_ge(s_cols, 1)
                pe.wait_ge(s_bvec, 1)
                pe.wait_ge(s_gelu, 2)
                for m in range(2):
                    mm = nc.tensor.matmul(ps[6][0:HD, 0:GROUPS * NC], w2[:, 0, m, :], hid[:, 0, m, :],
                                          start=m == 0, stop=m == 1)
                mm.then_inc(s_kvc, 1)
                pe.wait_ge(s_gelu, 4)
                for g in range(GROUPS):
                    for m in range(2):
                        mm = nc.tensor.matmul(ps[7][0:NC, g * HD:(g + 1) * HD], hid[:, 1, m, g * NC:(g + 1) * NC],
                                              w2[:, 1, m, :], start=m == 0, stop=m == 1)
                mm.then_inc(s_kvc, 1)

            def scores(s):
                kind, h, b, i = slots[s]
                bank = SCORE[s % 2]
                pe.wait_ge(s_evac, needed(slots[s]))
                if s >= 2:
                    pe.wait_ge(s_exp, s - 1)
                if s < 2:
                    pe.wait_ge(s_cmp_ready, 1)
                if kind == "cmp":
                    for hh in range(NSA_HEADS):
                        q = q_nsa[:, hh, i * P:(i + 1) * P]
                        o = bank[:, hh * NC:(hh + 1) * NC]
                        nc.tensor.matmul(o, q, kc_s[:, 0, hh // HEADS_PER_GROUP, :], start=True, stop=False)
                        mm = nc.tensor.matmul(o, q, kc_s[:, 1, hh // HEADS_PER_GROUP, :], start=False, stop=True)
                else:
                    n = (i + 1) * P
                    if kind == "nsa":
                        q = q_nsa[:, h, i * P:(i + 1) * P]
                        k_hi = k_nsa[:, 0, 2 * b + h // HEADS_PER_GROUP, 0:n]
                        k_lo = k_nsa[:, 1, 2 * b + h // HEADS_PER_GROUP, 0:n]
                    else:
                        q = q_diff[:, h % 2, b, i * P:(i + 1) * P]
                        k_hi, k_lo = k_diff[:, h % 2, 0, b, 0:n], k_diff[:, h % 2, 1, b, 0:n]
                    nc.tensor.matmul(bank[:, 0:n], q, k_hi, start=True, stop=False)
                    mm = nc.tensor.matmul(bank[:, 0:n], q, k_lo, start=False, stop=True)
                mm.then_inc(s_qk, 1)

            def turn_probs(s):
                if s not in turn:
                    return
                kind, h, b, i = slots[s]
                n = turn[s]
                if kind == "diff":
                    pe.wait_ge(s_comb, sum(1 for z in turned[:n + 1] if slots[z][0] == "diff"))
                else:
                    pe.wait_ge(s_exp, s + 1)
                if n >= 2:
                    pe.wait_ge(s_pt, n - 1)
                for j in range(2 if kind == "cmp" else i + 1):
                    mm = nc.tensor.transpose(TURN[n % 2][:, j * P:(j + 1) * P], E[:, s % E_SLOTS, j * P:(j + 1) * P],
                                             ident[:, :])
                mm.then_inc(s_turn, 1)

            def values(s):
                if s not in turn:
                    return
                kind, h, b, i = slots[s]
                n = turn[s]
                bank = OUTP[n % 2]
                pe.wait_ge(s_pt, n + 1)
                if n >= 2:
                    pe.wait_ge(s_of, n - 1)
                if kind == "cmp":
                    for g in range(GROUPS):
                        mm = nc.tensor.matmul(bank[:, g * 256:(g + 1) * 256], PT[:, n % 2, g * P:(g + 1) * P],
                                              vc_bd[:, g, :], start=True, stop=True)
                else:
                    g = h // HEADS_PER_GROUP
                    for j in range(i + 1):
                        v = v_nsa[:, b, j, g * HD:(g + 1) * HD] if kind == "nsa" else v_diff[:, h % 2, j, :]
                        mm = nc.tensor.matmul(bank[:, 0:v.shape[1]], PT[:, n % 2, j * P:(j + 1) * P], v,
                                              start=j == 0, stop=j == i)
                mm.then_inc(s_pv, 1)

            pe.wait_ge(s_ident, 16)
            pe.wait_ge(s_rows, 16 * 6)
            nc.tensor.transpose(ps[6][:, 0:N_ROWS], rows[0:N_ROWS, :], ident[0:N_ROWS, 0:N_ROWS]).then_inc(s_cols_t, 1)
            pe.wait_ge(s_btab, 16 * 3)
            nc.tensor.matmul(ps[7][0:NHEADS, 0:384], relb[:, :], choice[:, :], start=True, stop=True).then_inc(s_bvec_p, 1)

            turn_rows(0, lambda: pe.wait_ge(s_norm, NT))
            pe.wait_ge(s_tlo, KT)
            proj_chunk(0)
            proj_chunk(1)
            proj_chunk(2)
            hidden(0)
            proj_chunk(3)
            hidden(1)
            proj_chunk(4)
            compressed()
            for k in range(5, n_base):
                proj_chunk(k)

            upto = 0
            for s in range(n_slots + 3):
                if s < n_slots:
                    scores(s)
                    while upto < piece_upto[s]:
                        proj_piece(n_base + upto // PIECES, upto % PIECES)
                        upto += 1
                if 2 <= s < n_slots + 2:
                    turn_probs(s - 2)
                if s >= 3:
                    values(s - 3)

            turn_rows(1, lambda: pe.wait_ge(s_norm, 2 * NT))
            pe.wait_ge(s_tlo, 2 * KT)

            def rows_chunk(k, a_hi, a_lo, banks, first, last):
                kc = chunks[k][1][1]
                pe.wait_ge(s_split, k + 1)
                for kk in range(2):
                    hi, lo = wv_hi(k)[:, kk * 512:(kk + 1) * 512], wv_lo(k)[:, kk * 512:(kk + 1) * 512]
                    f = 2 * kc + kk
                    for t in range(NT):
                        mm = three(banks[t][:, :], a_hi[:, f, t * P:(t + 1) * P], a_lo[:, f, t * P:(t + 1) * P],
                                   hi, lo, first and kk == 0, last and kk == 1)
                mm.then_inc(s_chunk, 1)

            pe.wait_ge(s_of, len(turned))
            for dh in range(2):
                for kc in range(4):
                    rows_chunk(index[("o", (dh, kc))], xT_hi, xT_lo, FOUR[dh], kc == 0, kc == 3)

            pe.wait_ge(s_resid, 2 * NT)
            turn_rows(2, lambda: pe.wait_ge(s_norm, 3 * NT))
            pe.wait_ge(s_tlo, 3 * KT)
            for f in range(FT):
                for kind, bank, read in (("gate", PROJ[f % 2], s_silu), ("up", OUTP[f % 2], s_prod)):
                    k = index[(kind, f)]
                    pe.wait_ge(s_split, k + 1)
                    if f >= 2:
                        pe.wait_ge(read, f - 1)
                    for kt in range(KT):
                        hi, lo = wv_hi(k)[:, kt * P:(kt + 1) * P], wv_lo(k)[:, kt * P:(kt + 1) * P]
                        nc.tensor.matmul(bank[:, :], hi, xT_hi[:, kt, :], start=kt == 0, stop=False)
                        nc.tensor.matmul(bank[:, :], hi, xT_lo[:, kt, :], start=False, stop=False)
                        mm = nc.tensor.matmul(bank[:, :], lo, xT_hi[:, kt, :], start=False, stop=kt == KT - 1)
                    mm.then_inc(s_chunk, 1)
            for dh in range(2):
                for kc in range(FT // 2):
                    pe.wait_ge(s_alo, 2 * kc + 2 if dh == 0 else FT)
                    rows_chunk(index[("down", (dh, kc))], act_hi, act_lo, FOUR[1 - dh], kc == 0, kc == FT // 2 - 1)

        @block.scalar
        def _(act):
            n_pt = [0]

            def squares(stage):
                for t in range(NT):
                    if stage == 0:
                        act.wait_ge(s_x[t], 16)
                    elif stage == 1:
                        if t == 0:
                            act.wait_ge(s_of, len(turned))
                            act.wait_ge(s_tlo, KT)
                    else:
                        act.wait_ge(s_resid, (2 * NT if stage == 2 else 4 * NT) - NT + t + 1)
                    if stage * NT + t >= 2:
                        act.wait_ge(s_ss, stage * NT + t - 1)
                    if stage == 1:
                        nc.scalar.activation(junk(t)[:, 0:512], mix[:, t, 512:1024], ACT.Square,
                                             accum_out=stat[:, 16 + t:17 + t]).then_inc(s_ss, 1)
                    else:
                        nc.scalar.activation(junk(t) if stage < 3 else junk_late(t), xres[:, t, :], ACT.Square,
                                             accum_out=stat[:, 16 + t:17 + t]).then_inc(s_ss, 1)

            def junk(t):
                a = E[:, 0:2, :] if t % 2 == 0 else E[:, 2:4, :]
                return a.rearrange("p a b -> p (a b)")

            def junk_late(t):
                return (silu_g, prod)[t % 2][:, :, :].rearrange("p a b -> p (a b)")

            def root(stage, n):
                act.wait_ge(s_root_in, stage + 1)
                nc.scalar.activation(stat[:, 32:32 + n], stat[:, 0:n] if stage == 1 else stat[:, 16:16 + n],
                                     ACT.Sqrt).then_inc(s_root, 1)

            def split_hi(stage, gain):
                for kt in range(KT):
                    n = stage * KT + kt
                    act.wait_ge(s_tp, n + 1)
                    nc.scalar.activation(xT_hi[:, kt, :], ps[2 + kt % 4][:, :], ACT.Copy,
                                         scale=cols[:, gain(kt):gain(kt) + 1]).then_inc(s_thi, 1)

            def evac_hi(k):
                kind, a = chunks[k]
                if kind not in ("q", "k", "dq", "dk"):
                    return
                act.wait_ge(s_chunk, k + 1)
                if kind in ("dq", "dk") and a >= 2:
                    act.wait_ge(s_qk, last_diff_qk[a - 2] + 1)
                if kind == "dq" and a < 2:
                    act.wait_ge(s_gelu, 4)
                for hd in range(2):
                    src = PROJ[k % 2][hd * HD:(hd + 1) * HD, :]
                    if kind in ("q", "dq"):
                        dst = q_nsa[0:HD, 2 * a + hd, :] if kind == "q" else q_diff[0:HD, a % 2, hd, :]
                        ins = nc.scalar.activation(dst, src, ACT.Copy, scale=-SCALE)
                    else:
                        dst = (k_nsa[0:HD, 0, 2 * (a == "kw") + hd, :] if kind == "k"
                               else k_diff[0:HD, a % 2, 0, hd, :])
                        ins = nc.scalar.activation(dst, src, ACT.Copy)
                    ins.then_inc(s_hi, 1)

            def gelu(kv):
                for m in range(2):
                    act.wait_ge(s_w1, 4 * kv + 2 * m + 2)
                    nc.scalar.activation(hid[:, kv, m, :], ps[2 + 2 * kv + m][:, 0:GROUPS * NC],
                                         ACT.Gelu_apprx_tanh).then_inc(s_gelu, 1)

            def load_bias(n):
                h = bias_order[n]
                if n == 0:
                    act.wait_ge(s_spread, 16)
                if n >= BIAS_SLOTS:
                    act.wait_ge(s_add, bias_last[bias_order[n - BIAS_SLOTS]] + 1)
                base = bias_rows[h, 0, :]
                src = bass.AP(base.tensor, base.offset + 127, [[383, P], [1, 256]])
                act.dma_start(bias[:, n % BIAS_SLOTS, 256:512], src).then_inc(s_bias[n % BIAS_SLOTS], 16)

            def exps(s):
                kind, h, b, i = slots[s]
                n = 256 if kind == "cmp" else (i + 1) * P
                act.wait_ge(s_add, s + 1)
                if s >= E_SLOTS:
                    last = s - E_SLOTS
                    if last not in turn:
                        last += 1
                    act.wait_ge(s_turn, turns_upto[last])
                if kind == "cmp":
                    nc.scalar.activation(E[:, s % E_SLOTS, 0:n], SCORE[s % 2][:, 0:n], ACT.Exp, scale=-1.0).then_inc(s_exp, 1)
                else:
                    nc.scalar.activation(E[:, s % E_SLOTS, 0:n], SCORE[s % 2][:, 0:n], ACT.Exp, scale=-1.0,
                                         bias=nmax[:, s:s + 1], accum_out=ssum[:, s:s + 1]).then_inc(s_exp, 1)

            def copy_turned(s):
                if s not in turn:
                    return
                kind, h, b, i = slots[s]
                n = turn[s]
                w = 256 if kind == "cmp" else (i + 1) * P
                act.wait_ge(s_turn, n + 1)
                if n >= 2:
                    act.wait_ge(s_pv, n - 1)
                nc.scalar.copy(PT[:, n % 2, 0:w], TURN[n % 2][:, 0:w]).then_inc(s_pt, 1)

            act.dma_start(ident[:, :], c_ident).then_inc(s_ident, 16)
            act.dma_start(rows[0:8, :], norm1[0].rearrange("(k p) -> k p", p=P)).then_inc(s_rows, 16)
            act.dma_start(rows[8:16, :], norm2[0].rearrange("(k p) -> k p", p=P)).then_inc(s_rows, 16)
            act.dma_start(rows[16:17, :], diff_subln).then_inc(s_rows, 16)
            act.dma_start(rows[17:21, :], nsa_norm[0].rearrange("(k p) -> k p", p=P)).then_inc(s_rows, 16)
            act.dma_start(rows[21:37, :], cmp_pos_k[0].rearrange("(j l) d -> j (l d)", l=2)).then_inc(s_rows, 16)
            act.dma_start(rows[37:53, :], cmp_pos_v[0].rearrange("(j l) d -> j (l d)", l=2)).then_inc(s_rows, 16)
            act.dma_start(relb[:, :], rel_bias).then_inc(s_btab, 16)
            act.dma_start(choice[:, :], c_choice).then_inc(s_btab, 16)
            act.dma_start(causal[:, :], c_causal).then_inc(s_btab, 16)
            squares(0)
            root(0, NT)
            for n, v in enumerate((lambda_q1, lambda_k1, lambda_q2, lambda_k2)):
                act.dma_start(lam_in[:, n, :], v[0].partition_broadcast(P)).then_inc(s_lamin, 16)
            for n, v in enumerate((cmp_w2_k, cmp_w2_v)):
                act.dma_start(w2[:, n, :, :], v[0].rearrange("(m p) d -> p m d", p=P)).then_inc(s_small, 16)
            act.dma_start(cmask[:, :, :], c_cmask).then_inc(s_small, 16)
            act.dma_start(has_cmp[:, :], c_has).then_inc(s_small, 16)
            act.wait_ge(s_cols, 1)
            split_hi(0, lambda kt: C_N1 + kt)
            act.wait_ge(s_bvec, 1)
            act.dma_start(bias_scratch[:, :], bias_vec[:, :]).then_inc(s_scratch, 16)
            act.wait_ge(s_scratch, 16)
            act.dma_start(bias_rows[:, :, :], bias_scratch[:, :].unsqueeze(1).to_broadcast([NHEADS, P, 384])).then_inc(s_spread, 16)
            act.wait_ge(s_lamdot, 1)
            nc.scalar.activation(lam[:, 2:4], lam[:, 0:2], ACT.Exp).then_inc(s_lamexp, 1)
            load_bias(0)
            load_bias(1)
            evac_hi(2)
            gelu(0)
            gelu(1)
            evac_hi(4)
            act.wait_ge(s_kvc, 1)
            nc.scalar.copy(kc_s[0:HD, 0, :, :].rearrange("p g n -> p (g n)"), ps[6][0:HD, 0:GROUPS * NC]).then_inc(s_kchi, 1)
            act.wait_ge(s_gexp_in, 1)
            nc.scalar.activation(gates[:, :, :], gates[:, :, :], ACT.Exp, scale=-1.0).then_inc(s_gexp, 1)
            for k in range(5, n_base):
                evac_hi(k)

            for s in range(n_slots + 3):
                if s < n_slots:
                    for n in range(2, NHEADS):
                        if s == bias_first[bias_order[n - 1]]:
                            load_bias(n)
                    exps(s)
                    for k in chunks_done_in[s]:
                        evac_hi(k)
                if 2 <= s < n_slots + 2:
                    copy_turned(s - 2)

            squares(1)
            root(1, 20)
            split_hi(1, lambda kt: C_SUB if kt < 4 else C_NSA + kt - 4)
            squares(2)
            root(2, NT)
            split_hi(2, lambda kt: C_N2 + kt)
            act.dma_start(final_g[:, :], final_norm.partition_broadcast(P)).then_inc(s_lamin, 16)
            for f in range(FT):
                act.wait_ge(s_chunk, index[("gate", f)] + 1)
                if f >= 2:
                    act.wait_ge(s_prod, f - 1)
                nc.scalar.activation(silu_g[:, f % 2, :], PROJ[f % 2][:, :], ACT.Silu).then_inc(s_silu, 1)
                act.wait_ge(s_prod, f + 1)
                nc.scalar.copy(act_hi[:, f, :], prod[:, f % 2, :]).then_inc(s_ahi, 1)
            squares(3)
            root(3, NT)

        @block.vector
        def _(dve):
            chain = [0]

            def link(ins):
                chain[0] += 1
                ins.then_inc(s_dve, 1)
                dve.wait_ge(s_dve, chain[0])

            def norm_rows(stage):
                dve.wait_ge(s_ss, (stage + 1) * NT)
                if stage == 1:
                    link(nc.vector.tensor_scalar(stat[:, 0:16], stat[:, 0:16], 1.0 / P, EPS, ALU.mult, ALU.add))
                    nc.vector.tensor_scalar(stat[:, 16:20], stat[:, 16:20], 1.0 / 512, EPS, ALU.mult, ALU.add).then_inc(s_root_in, 1)
                else:
                    nc.vector.tensor_scalar(stat[:, 16:20], stat[:, 16:20], 1.0 / D, EPS, ALU.mult, ALU.add).then_inc(s_root_in, 1)
                dve.wait_ge(s_root, stage + 1)
                n = 20 if stage == 1 else NT
                link(nc.vector.reciprocal(stat[:, 32:32 + n], stat[:, 32:32 + n]))

            def scale_rows(stage):
                for t in range(NT):
                    if stage == 1:
                        for h in range(DIFF_HEADS):
                            c = 32 + 4 * t + h
                            m = mix[:, t, h * P:(h + 1) * P]
                            nc.vector.tensor_scalar(m, m, stat[:, c:c + 1], None, ALU.mult)
                        m = mix[:, t, 512:1024]
                        nc.vector.tensor_scalar(m, m, stat[:, 48 + t:49 + t], None, ALU.mult).then_inc(s_norm, 1)
                    else:
                        nc.vector.tensor_scalar(mix[:, t, :], xres[:, t, :], stat[:, 32 + t:33 + t], None, ALU.mult).then_inc(s_norm, 1)

            def split_lo(stage, gain):
                for kt in range(KT):
                    n = stage * KT + kt
                    dve.wait_ge(s_thi, n + 1)
                    nc.vector.scalar_tensor_tensor(out=xT_lo[:, kt, :], in0=ps[2 + kt % 4][:, :],
                                                   scalar=cols[:, gain(kt):gain(kt) + 1],
                                                   in1=xT_hi[:, kt, :].bitcast(F32),
                                                   op0=ALU.mult, op1=ALU.subtract).then_inc(s_tlo, 1)

            def evac(k):
                kind, a = chunks[k]
                bank = PROJ[k % 2]
                dve.wait_ge(s_chunk, k + 1)
                if kind == "c":
                    for par in range(2):
                        for g in range(GROUPS):
                            src = bank[g * HD:(g + 1) * HD, :]
                            src = bass.AP(src.tensor, src.offset + par, [src.ap[0], [2, 16], [CMP_STRIDE, N_CMP]])
                            pos = cols[par * HD:(par + 1) * HD, C_POS + 16 * a:C_POS + 16 * a + 16]
                            ins = nc.vector.tensor_tensor(blk[a][par * HD:(par + 1) * HD, :, g, 0:N_CMP], src,
                                                          pos.unsqueeze(2).to_broadcast([HD, 16, N_CMP]), ALU.add)
                elif kind in ("v", "dv"):
                    if kind == "v":
                        dst = v_nsa[:, int(a == "vw"), :, :]
                    else:
                        if a >= 2:
                            dve.wait_ge(s_pv, turn[last_diff_qk[a - 2]] + 1)
                        dst = v_diff[:, a % 2, :, :]
                    ins = nc.vector.tensor_copy(dst.rearrange("p t n -> p (t n)"), bank[:, :])
                elif kind == "g":
                    nc.vector.tensor_copy(gates[:, :, :].rearrange("p t n -> p (t n)"), bank[:, 0:NT * GATES]).then_inc(s_gexp_in, 1)
                    dve.wait_ge(s_gexp, 1)
                    link(nc.vector.tensor_scalar(gates[:, :, :], gates[:, :, :], 1.0, None, ALU.add))
                    ins = nc.vector.reciprocal(gates[:, :, :], gates[:, :, :])
                else:
                    for hd in range(2):
                        src = bank[hd * HD:(hd + 1) * HD, :]
                        dve.wait_ge(s_hi, hi_upto[k] - 1 + hd)
                        if kind in ("q", "dq"):
                            q = q_nsa[:, 2 * a + hd, :] if kind == "q" else q_diff[:, a % 2, hd, :]
                            ins = nc.vector.scalar_tensor_tensor(out=q[HD:P, :], in0=src, scalar=-SCALE,
                                                                 in1=q[0:HD, :].bitcast(F32),
                                                                 op0=ALU.mult, op1=ALU.subtract)
                        else:
                            if kind == "k":
                                hi, lo = (k_nsa[:, z, 2 * (a == "kw") + hd, :] for z in range(2))
                            else:
                                hi, lo = (k_diff[:, a % 2, z, hd, :] for z in range(2))
                            link(nc.vector.tensor_tensor(lo[0:HD, :], src, hi[0:HD, :].bitcast(F32), ALU.subtract))
                            nc.vector.tensor_copy(hi[HD:P, :], hi[0:HD, :])
                            ins = nc.vector.tensor_copy(lo[HD:P, :], lo[0:HD, :])
                ins.then_inc(s_evac, 1)

            def add_bias(s):
                kind, h, b, i = slots[s]
                bank = SCORE[s % 2]
                dve.wait_ge(s_qk, s + 1)
                if kind == "cmp":
                    z = bank[:, 0:NSA_HEADS * NC].rearrange("p (h n) -> p h n", n=NC)
                    link(nc.vector.tensor_tensor(z, z, cmask[:, i, :].unsqueeze(1).to_broadcast([P, NSA_HEADS, NC]), ALU.add))
                    link(nc.vector.tensor_reduce(cstat[:, i, 0, :], z, AX.X, ALU.min))
                    nc.vector.tensor_tensor(z, z, cstat[:, i, 0, :].unsqueeze(2).to_broadcast([P, NSA_HEADS, NC]),
                                            ALU.subtract).then_inc(s_add, 1)
                    return
                n = (i + 1) * P
                m = bias_order.index(bias_head(slots[s]))
                dve.wait_ge(s_bias[m % BIAS_SLOTS], 16 * (m // BIAS_SLOTS + 1))
                nc.vector.tensor_tensor_reduce(out=bank[:, 0:n], in0=bank[:, 0:n],
                                               in1=bias[:, m % BIAS_SLOTS, 512 - n:512], scale=1.0, scalar=3.0e38,
                                               op0=ALU.add, op1=ALU.min, accum_out=nmax[:, s:s + 1]).then_inc(s_add, 1)

            def weigh(s):
                kind, h, b, i = slots[s]
                dve.wait_ge(s_exp, s + 1)
                if kind == "cmp":
                    z = E[:, s % E_SLOTS, 0:256].rearrange("p (h n) -> p h n", n=NC)
                    link(nc.vector.tensor_reduce(cstat[:, i, 1, :], z, AX.X, ALU.add))
                    link(nc.vector.reciprocal(cstat[:, i, 2, :], cstat[:, i, 1, :]))
                    g0 = gates[:, i, :].rearrange("p (h c) -> p h c", c=3)[:, :, 0]
                    link(nc.vector.scalar_tensor_tensor(out=cstat[:, i, 3, :], in0=g0, scalar=has_cmp[:, i:i + 1],
                                                        in1=cstat[:, i, 2, :], op0=ALU.mult, op1=ALU.mult))
                    return
                link(nc.vector.reciprocal(ssum[:, s:s + 1], ssum[:, s:s + 1]))
                if kind == "nsa":
                    c = 3 * h + 1 + b
                    nc.vector.tensor_tensor(coef[:, s:s + 1], ssum[:, s:s + 1], gates[:, i, c:c + 1], ALU.mult).then_inc(s_coefs, 1)
                elif b == 1:
                    n = (i + 1) * P
                    e0, e1 = E[:, (s - 1) % E_SLOTS, 0:n], E[:, s % E_SLOTS, 0:n]
                    link(nc.vector.tensor_scalar(e1, e1, ssum[:, s:s + 1], lam[:, 6:7], ALU.mult, ALU.mult))
                    nc.vector.scalar_tensor_tensor(out=e1, in0=e0, scalar=ssum[:, s - 1:s], in1=e1,
                                                   op0=ALU.mult, op1=ALU.add).then_inc(s_comb, 1)

            def gather(s):
                if s not in turn:
                    return
                kind, h, b, i = slots[s]
                n = turn[s]
                bank = OUTP[n % 2]
                dve.wait_ge(s_pv, n + 1)
                if kind == "nsa":
                    dve.wait_ge(s_coefs, sum(1 for z in turned[:n + 1] if slots[z][0] == "nsa"))
                    m = mix[:, i, 512 + h * HD:512 + (h + 1) * HD]
                    if b == 0:
                        nc.vector.tensor_scalar(m, bank[:, 0:HD], coef[:, s:s + 1], None, ALU.mult).then_inc(s_of, 1)
                    else:
                        dve.wait_ge(s_of, n)
                        nc.vector.scalar_tensor_tensor(out=m, in0=bank[:, 0:HD], scalar=coef[:, s:s + 1], in1=m,
                                                       op0=ALU.mult, op1=ALU.add).then_inc(s_of, 1)
                elif kind == "diff":
                    m = mix[:, i, h * P:(h + 1) * P]
                    nc.vector.tensor_copy(m, bank[:, 0:P]).then_inc(s_of, 1)
                    dve.wait_ge(s_of, n + 1)
                    c = 4 * i + h
                    link(nc.vector.tensor_tensor_reduce(out=sq[:, 0:P], in0=m, in1=m, scale=1.0, scalar=0.0, op0=ALU.mult,
                                                        op1=ALU.add, accum_out=stat[:, c:c + 1]))
                else:
                    z = bank[:, :].rearrange("p (h n) -> p h n", n=HD)
                    link(nc.vector.tensor_tensor(sq[:, :].rearrange("p (h n) -> p h n", n=HD), z,
                                                 cstat[:, i, 3, :].unsqueeze(2).to_broadcast([P, NSA_HEADS, HD]), ALU.mult))
                    m = mix[:, i, 512:1024]
                    nc.vector.tensor_tensor(m, m, sq[:, :], ALU.add).then_inc(s_of, 1)
                    dve.wait_ge(s_of, n + 1)

            nc.vector.memset(bias[:, :, 0:256], 0.0)
            nc.vector.memset(vc_bd[:, :, :], 0.0)
            for kv in range(2):
                nc.vector.memset(blk[kv][:, :, :, N_CMP:NC], 0.0)
            link(nc.vector.memset(sq[:, :], 0.0))
            norm_rows(0)
            scale_rows(0)
            dve.wait_ge(s_cols_t, 1)
            link(nc.vector.tensor_copy(cols[:, 0:N_ROWS], ps[6][:, 0:N_ROWS]))
            nc.vector.tensor_scalar(cols[:, C_SUB:C_SUB + 1], cols[:, C_SUB:C_SUB + 1], 1.0 - LAMBDA_INIT, None,
                                    ALU.mult).then_inc(s_cols, 1)
            dve.wait_ge(s_bvec_p, 1)
            nc.vector.tensor_tensor(bias_vec[:, :], ps[7][0:NHEADS, 0:384], causal[:, :], ALU.add).then_inc(s_bvec, 1)
            dve.wait_ge(s_cols, 1)
            split_lo(0, lambda kt: C_N1 + kt)
            dve.wait_ge(s_lamin, 16 * 4)
            for n in range(2):
                ins = nc.vector.tensor_tensor_reduce(out=sq[:, n * HD:(n + 1) * HD], in0=lam_in[:, 2 * n, :],
                                                     in1=lam_in[:, 2 * n + 1, :], scale=1.0, scalar=0.0, op0=ALU.mult,
                                                     op1=ALU.add, accum_out=lam[:, n:n + 1])
            ins.then_inc(s_lamdot, 1)
            dve.wait_ge(s_lamexp, 1)
            link(nc.vector.tensor_tensor(lam[:, 5:6], lam[:, 3:4], lam[:, 2:3], ALU.subtract))
            link(nc.vector.tensor_scalar(lam[:, 6:7], lam[:, 5:6], -LAMBDA_INIT, None, ALU.add))
            for k in range(5):
                evac(k)
            dve.wait_ge(s_kchi, 1)
            k_hi, k_lo = (kc_s[:, z, :, :].rearrange("p g n -> p (g n)") for z in range(2))
            link(nc.vector.tensor_tensor(k_lo[0:HD, :], ps[6][0:HD, 0:GROUPS * NC], k_hi[0:HD, :].bitcast(F32), ALU.subtract))
            nc.vector.tensor_copy(k_hi[HD:P, :], k_hi[0:HD, :])
            nc.vector.tensor_copy(k_lo[HD:P, :], k_lo[0:HD, :])
            dve.wait_ge(s_kvc, 2)
            for g in range(GROUPS):
                for hh in range(HEADS_PER_GROUP):
                    ins = nc.vector.tensor_copy(vc_bd[hh * NC:(hh + 1) * NC, g, hh * HD:(hh + 1) * HD],
                                                ps[7][0:NC, g * HD:(g + 1) * HD])
            ins.then_inc(s_cmp_ready, 1)
            for k in range(5, n_base):
                evac(k)

            for s in range(n_slots + 3):
                if s < n_slots:
                    add_bias(s)
                if 1 <= s < n_slots + 1:
                    weigh(s - 1)
                if s < n_slots:
                    for k in chunks_done_in[s]:
                        evac(k)
                if s >= 3:
                    gather(s - 3)

            norm_rows(1)
            scale_rows(1)
            split_lo(1, lambda kt: C_SUB if kt < 4 else C_NSA + kt - 4)

            def add_residual(kind, n_kc, dh, banks):
                dve.wait_ge(s_chunk, index[(kind, (dh, n_kc - 1))] + 1)
                for t in range(NT):
                    z = xres[:, t, dh * 512:(dh + 1) * 512]
                    nc.vector.tensor_tensor(z, z, banks[t][:, :], ALU.add).then_inc(s_resid, 1)

            for dh in range(2):
                add_residual("o", 4, dh, FOUR[dh])
            norm_rows(2)
            scale_rows(2)
            split_lo(2, lambda kt: C_N2 + kt)
            for f in range(FT):
                dve.wait_ge(s_silu, f + 1)
                dve.wait_ge(s_chunk, index[("up", f)] + 1)
                if f >= 2:
                    dve.wait_ge(s_ahi, f - 1)
                nc.vector.tensor_tensor(prod[:, f % 2, :], silu_g[:, f % 2, :], OUTP[f % 2][:, :], ALU.mult).then_inc(s_prod, 1)
                dve.wait_ge(s_ahi, f + 1)
                nc.vector.tensor_tensor(act_lo[:, f, :], prod[:, f % 2, :], act_hi[:, f, :].bitcast(F32),
                                        ALU.subtract).then_inc(s_alo, 1)
            for dh in range(2):
                add_residual("down", FT // 2, dh, FOUR[1 - dh])
            norm_rows(3)
            dve.wait_ge(s_lamin, 16 * 5)
            for t in range(NT):
                nc.vector.scalar_tensor_tensor(out=xres[:, t, :], in0=xres[:, t, :], scalar=stat[:, 32 + t:33 + t],
                                               in1=final_g[:, :], op0=ALU.mult, op1=ALU.mult).then_inc(s_y, 1)


_INS = ["x", "norm1", "w_in", "lambda_q1", "lambda_k1", "lambda_q2", "lambda_k2", "diff_subln",
        "cmp_pos_k", "cmp_w1_k", "cmp_w2_k", "cmp_pos_v", "cmp_w1_v", "cmp_w2_v", "nsa_norm",
        "w_out", "norm2", "w_gate", "w_up", "w_down", "rel_bias", "final_norm"]


def kernel(**inputs):
    import concourse.bacc as _bacc
    from concourse.bass_utils import run_bass_kernel_spmd as _run

    nc = _bacc.Bacc("TRN2", target_bir_lowering=False, num_devices=1)
    arrays, args = {}, []
    for name in _INS:
        arrays[f"in_{name}_dram"] = np.ascontiguousarray(inputs[name])
    for name, a in shape_constants().items():
        arrays[f"in_{name}_dram"] = np.ascontiguousarray(a)
    for name, a in arrays.items():
        args.append(nc.dram_tensor(name, a.shape, mybir.dt.from_np(a.dtype), kind="ExternalInput").ap())
    args.append(nc.dram_tensor("bias_scratch", (NHEADS, 384), F32).ap())
    args.append(nc.dram_tensor("bias_rows", (NHEADS, P, 384), F32).ap())
    args.append(nc.dram_tensor("out_0_dram", (1, T, D), F32, kind="ExternalOutput").ap())
    hymba_block(nc, *args)
    r = _run(nc, [arrays], core_ids=[0])
    return r.results[0]["out_0_dram"]
```

```python
import math
from contextlib import ExitStack

import numpy as np

import concourse.bass as bass
from concourse import mybir

F32 = mybir.dt.float32
F32R = mybir.dt.float32r
ALU = mybir.AluOpType
ACT = mybir.ActivationFunctionType
AX = mybir.AxisListType

P = 128
D = 1024
T = 512
NT = T // P
KT = D // P
DIFF_HEADS, HD = 4, 64
NSA_HEADS, GROUPS = 8, 2
HEADS_PER_GROUP = NSA_HEADS // GROUPS
NHEADS = DIFF_HEADS + NSA_HEADS
N_BUCKETS, MAX_DISTANCE = 32, 128
CMP_LEN, CMP_STRIDE, CMP_HIDDEN = 32, 16, 256
N_CMP = (T - CMP_LEN) // CMP_STRIDE + 1
NC = 32
D_FF = 2816
FT = D_FF // P
EPS = 1e-6
WARM = 16
NEG = 1e30
SCALE = HD ** -0.5
LAMBDA_INIT = 0.8 - 0.6 * math.exp(0.0)
COL = {"dq": 0, "dk": 512, "dv": 1024, "nq": 1536, "kc": 2048, "vc": 2176, "ksl": 2304, "vsl": 2432,
       "kw": 2560, "vw": 2688, "gt": 2816}
GATES = 24

RAW_SLOTS = 3
SPLIT_SLOTS = 4
E_SLOTS = 4
BIAS_SLOTS = 3
PIECES = 8
PIECES_PER_SLOT = 1.26
LEAD_PIECES = 6
V_COLS = 2 * P + GATES
SLOT = 4 * V_COLS
OUT_ORDER = (2, 3, 0, 1)
MIX_ORDER = (4, 5, 6, 7, 0, 1, 2, 3)


def shape_constants():
    ident = np.eye(P, dtype=np.float32)
    dist = 255 - np.arange(384)
    half = N_BUCKETS // 2
    pos = np.maximum(dist, 1).astype(np.float32)
    far = half + (np.log(pos / half) / math.log(MAX_DISTANCE / half) * (N_BUCKETS - half)).astype(np.int32)
    bucket = np.where(dist < half, np.maximum(dist, 0), np.minimum(far, N_BUCKETS - 1))
    choice = np.zeros((N_BUCKETS, 384), np.float32)
    for j in range(384):
        if dist[j] >= 0:
            choice[bucket[j], j] -= 1.0
            choice[N_BUCKETS - 1, j] += 1.0
    causal = np.broadcast_to(np.where(dist < 0, np.float32(NEG), np.float32(0)), (NHEADS, 384))
    q = np.arange(T)[:, None]
    n = np.arange(NC)[None, :]
    hidden = (n * CMP_STRIDE + CMP_LEN - 1 > q) | (n >= N_CMP)
    cmask = np.where(hidden, np.float32(NEG), np.float32(0)).reshape(NT, P, NC).transpose(1, 0, 2)
    has = (np.arange(T) >= CMP_LEN - 1).astype(np.float32).reshape(NT, P).T
    return {"c_ident": ident, "c_choice": choice, "c_causal": np.ascontiguousarray(causal),
            "c_cmask": np.ascontiguousarray(cmask), "c_has": np.ascontiguousarray(has)}


def plan_chunks():
    chunks = [("c", 0), ("c", 1), ("k", "ksl"), ("vg", 0), ("vg", 1), ("k", "kw"), ("q", 0)]
    base = len(chunks)
    chunks += [("q", 1), ("dq", 0), ("dk", 0), ("dv", (0, 0)), ("dv", (0, 1)), ("q", 2), ("dq", 1), ("dk", 1),
               ("q", 3), ("dq", 2), ("dk", 2), ("dv", (1, 0)), ("dv", (1, 1)), ("dq", 3), ("dk", 3)]
    proj = len(chunks)
    chunks += [("o", (dh, kc)) for dh in range(2) for kc in OUT_ORDER]
    for f in range(FT):
        chunks += [("gate", f), ("up", f)]
    chunks += [("down", (dh, kc)) for dh in range(2) for kc in range(FT // 2)]
    return chunks, base, proj


def plan_slots():
    slots = []

    def nsa(pair):
        for h in (2 * pair, 2 * pair + 1):
            for b in range(2):
                slots.extend(("nsa", h, b, i) for i in range(NT))

    def diff(h):
        slots.extend(("diff", h, m, i) for i in range(NT) for m in range(2))

    nsa(0), nsa(1), diff(0), nsa(2), diff(1), nsa(3)
    slots.extend(("cmp", 0, 0, t) for t in range(NT))
    diff(2), diff(3)
    return slots


def hymba_block(nc, x, norm1, w_in, lambda_q1, lambda_k1, lambda_q2, lambda_k2, diff_subln,
                cmp_pos_k, cmp_w1_k, cmp_w2_k, cmp_pos_v, cmp_w1_v, cmp_w2_v, nsa_norm,
                w_out, norm2, w_gate, w_up, w_down, rel_bias, final_norm,
                c_ident, c_choice, c_causal, c_cmask, c_has, bias_scratch, bias_rows, out):
    chunks, n_base, n_proj = plan_chunks()
    slots = plan_slots()
    n_slots = len(slots)
    index = {c: k for k, c in enumerate(chunks)}

    w1_after = {1: [(0, 0)], 2: [(1, 0)], 3: [(0, 1), (1, 1)], 4: [(0, 2), (1, 2)], 5: [(0, 3), (1, 3)]}
    raws = []
    for k, c in enumerate(chunks):
        raws.append(("chunk", k))
        if c == ("vg", 0):
            continue
        raws += [("w1", a) for a in (w1_after[k - 1] if c == ("vg", 1) else []) + w1_after.get(k, [])]
    raw_of = {r: n for n, r in enumerate(raws)}
    w1_order = [r[1] for r in raws if r[0] == "w1"]

    def needed(slot):
        kind, h, _, _ = slot
        if kind == "diff":
            return index[("dk", h)] + 1 if h else index[("dv", (0, 1))] + 1
        return index[("q", 3 if kind == "cmp" else h // 2)] + 1

    n_pieces = (n_proj - n_base) * PIECES
    piece_upto, done = [], 0
    for s in range(n_slots):
        ahead = min(s + 2, n_slots - 1)
        done = max(done, min(n_pieces, LEAD_PIECES + int(PIECES_PER_SLOT * (s + 1))), (needed(slots[ahead]) - n_base) * PIECES)
        piece_upto.append(done)
    chunks_done_in = [[] for _ in range(n_slots)]
    for k in range(n_base, n_proj):
        s = next(s for s in range(n_slots) if piece_upto[s] >= (k - n_base + 1) * PIECES)
        chunks_done_in[s].append(k)

    turned = [s for s in range(n_slots) if not (slots[s][0] == "diff" and slots[s][2] == 0)]
    turn = {s: n for n, s in enumerate(turned)}
    turns_upto = [sum(1 for x_ in turned if x_ <= s) for s in range(n_slots)]

    def release(k):
        return k + 1 if chunks[k][0] in ("vg", "dv") and chunks[k + 1][0] == chunks[k][0] and k + 1 < n_proj \
            and (chunks[k][1] == 0 or (chunks[k][0] == "dv" and chunks[k][1][1] == 0)) else k

    early = max(i for i, x_ in enumerate(slots) if x_[0] == "cmp") + 5
    cmp_last = early - 5
    early_norm = early + 3

    def bias_head(slot):
        return slot[1] if slot[0] == "diff" else DIFF_HEADS + slot[1]

    bias_order = []
    for s in slots:
        if s[0] != "cmp" and bias_head(s) not in bias_order:
            bias_order.append(bias_head(s))
    bias_first = {h: min(i for i, s in enumerate(slots) if s[0] != "cmp" and bias_head(s) == h) for h in bias_order}
    bias_last = {h: max(i for i, s in enumerate(slots) if s[0] != "cmp" and bias_head(s) == h) for h in bias_order}
    last_diff_qk = {h: max(i for i, s in enumerate(slots) if s[0] == "diff" and s[1] == h) for h in range(DIFF_HEADS)}

    hi_upto, n_hi = [], 0
    for c in chunks[:n_proj]:
        if c[0] in ("q", "k", "dq", "dk"):
            n_hi += 2
        hi_upto.append(n_hi)

    with ExitStack() as ctx:
        def sem(name):
            return ctx.enter_context(nc.semaphore(name))

        def sb(name, shape, dt=F32, stack=ctx):
            return stack.enter_context(nc.sbuf_tensor(name, shape, dt))

        ps = [ctx.enter_context(nc.psum_tensor(f"bank{b}", [P, 512], F32)) for b in range(8)]
        PROJ, SCORE, TURN, OUTP = ps[0:2], ps[2:4], ps[4:6], ps[6:8]
        FOUR = [[ps[0], ps[1], ps[6], ps[7]], [ps[2], ps[3], ps[4], ps[5]]]

        ident = sb("ident", [P, P])
        rows = sb("rows", [P, P])
        cols = sb("cols", [P, 56])
        relb = sb("relb", [N_BUCKETS, NHEADS])
        cmask = sb("cmask", [P, NT, NC])
        has_cmp = sb("has_cmp", [P, NT])
        lam = sb("lam", [P, 8])
        w2 = sb("w2", [P, 2, 2, HD])
        stat = sb("stat", [P, 64])
        gates = sb("gates", [P, NT, GATES])
        ones = sb("ones", [P, P])
        nmax = sb("nmax", [P, n_slots])
        ssum = sb("ssum", [P, n_slots])
        coef = sb("coef", [P, n_slots])
        cstat = sb("cstat", [P, NT, 4, NSA_HEADS])
        sq = sb("sq", [P, 512])
        xres = sb("xres", [P, NT, D])
        xT_hi = sb("xT_hi", [P, KT, T], F32R)
        xT_lo = sb("xT_lo", [P, KT, T], F32R)
        raw = sb("raw", [P, RAW_SLOTS, SLOT])
        w_hi = sb("w_hi", [P, SPLIT_SLOTS, SLOT], F32R)
        w_lo = sb("w_lo", [P, SPLIT_SLOTS, SLOT], F32R)

        with ExitStack() as attention:
            mix = sb("mix", [P, NT, D], F32, attention)
            with ExitStack() as mixed:
                mixT_hi = sb("mixT_hi", [P, KT, T], F32R, mixed)
                mixT_lo = sb("mixT_lo", [P, KT, T], F32R, mixed)
            q_nsa = sb("q_nsa", [P, NSA_HEADS, T], F32R, attention)
            k_nsa = sb("k_nsa", [P, 2, 2 * GROUPS, T], F32R, attention)
            v_nsa = sb("v_nsa", [P, 2, NT, P], F32, attention)
            v_diff = sb("v_diff", [P, NT, 2 * P], F32, attention)
            bias = sb("bias", [P, BIAS_SLOTS, 512], F32, attention)
            E = sb("E", [P, E_SLOTS, 512], F32, attention)
            PT = sb("PT", [P, 2, 512], F32, attention)
            kc_s = sb("kc_s", [P, 2, GROUPS, NC], F32R, attention)
            vc_bd = sb("vc_bd", [P, GROUPS, 4 * HD], F32, attention)
            hid = sb("hid", [P, 2, 2, GROUPS * NC], F32, attention)
            hid_rows = sb("hid_rows", [GROUPS * NC, 2, CMP_HIDDEN], F32, attention)
            with ExitStack() as compress:
                blk = [sb(f"blk{i}", [P, 16, GROUPS, NC], F32, compress) for i in range(2)]
                choice = sb("choice", [N_BUCKETS, 384], F32, compress)
                causal = sb("causal", [NHEADS, 384], F32, compress)
                bias_vec = sb("bias_vec", [NHEADS, 384], F32, compress)
                lam_in = sb("lam_in", [P, 4, HD], F32, compress)
            q_diff = sb("q_diff", [P, 2, 2, T], F32R, attention)
            k_diff = sb("k_diff", [P, 2, 2, 2, T], F32R, attention)
        with ExitStack() as swiglu:
            act_hi = sb("act_hi", [P, FT, T], F32R, swiglu)
            act_lo = sb("act_lo", [P, FT, T], F32R, swiglu)
            final_g = sb("final_g", [P, D], F32, swiglu)
            norm_b = sb("norm_b", [P, T], F32, swiglu)
            diag = sb("diag", [P, T], F32, swiglu)
            gate_n = sb("gate_n", [P, 2, T], F32, swiglu)
            up_n = sb("up_n", [P, 2, T], F32, swiglu)

        s_x = [sem(f"s_x{t}") for t in range(NT)]
        s_ident, s_rows, s_btab, s_small, s_lamin = sem("s_ident"), sem("s_rows"), sem("s_btab"), sem("s_small"), sem("s_lamin")
        s_final_g = sem("s_final_g")
        s_raw = [sem(f"s_raw{i}") for i in range(RAW_SLOTS)]
        s_bias = [sem(f"s_bias{i}") for i in range(BIAS_SLOTS)]
        s_scratch, s_spread = sem("s_scratch"), sem("s_spread")
        s_whi, s_split = sem("s_whi"), sem("s_split")
        s_chunk = sem("s_chunk")
        s_w1 = sem("s_w1")
        s_cols_t, s_cols = sem("s_cols_t"), sem("s_cols")
        s_bvec_p, s_bvec = sem("s_bvec_p"), sem("s_bvec")
        s_ss, s_root_in, s_root, s_norm = sem("s_ss"), sem("s_root_in"), sem("s_root"), sem("s_norm")
        s_tp, s_thi, s_tlo = sem("s_tp"), sem("s_thi"), sem("s_tlo")
        s_hi, s_evac = sem("s_hi"), sem("s_evac")
        s_gexp = sem("s_gexp")
        s_lamdot, s_lamexp = sem("s_lamdot"), sem("s_lamexp")
        s_hid, s_gelu, s_hid_t, s_hid_c = sem("s_hid"), sem("s_gelu"), sem("s_hid_t"), sem("s_hid_c")
        s_kvc, s_kchi, s_cmp_ready = sem("s_kvc"), sem("s_kchi"), sem("s_cmp_ready")
        s_zero, s_ones = sem("s_zero"), sem("s_ones")
        s_qk, s_add, s_exp, s_comb = sem("s_qk"), sem("s_add"), sem("s_exp"), sem("s_comb")
        s_turn, s_pt, s_pv, s_of = sem("s_turn"), sem("s_pt"), sem("s_pv"), sem("s_of")
        s_coefs, s_resid = sem("s_coefs"), sem("s_resid")
        s_gn, s_un, s_diag, s_nb_t, s_nb = sem("s_gn"), sem("s_un"), sem("s_diag"), sem("s_nb_t"), sem("s_nb")
        s_last, s_gx = sem("s_last"), sem("s_gx")
        s_silu, s_prod, s_ahi, s_alo = sem("s_silu"), sem("s_prod"), sem("s_ahi"), sem("s_alo")
        s_y, s_ya, s_final, s_out = sem("s_y"), sem("s_ya"), sem("s_final"), sem("s_out")
        s_dve = sem("s_dve")

        C_N1, C_N2, C_SUB, C_NSA, C_POS = 0, 8, 16, 17, 21
        N_ROWS = 53

        def wv_hi(k):
            return w_hi[:, k % SPLIT_SLOTS, :]

        def wv_lo(k):
            return w_lo[:, k % SPLIT_SLOTS, :]

        def chunk_src(k):
            kind, a = chunks[k]
            if kind in ("o", "down"):
                w = w_out if kind == "o" else w_down
                dh, kc = a
                return w[0].rearrange("(k p) n -> p k n", p=P)[:, 2 * kc:2 * kc + 2, 512 * dh:512 * dh + 512]
            if kind in ("gate", "up"):
                w, c0 = (w_gate if kind == "gate" else w_up), P * a
            elif kind == "c":
                w, c0 = w_in, COL["kc" if a == 0 else "vc"]
            elif kind == "k":
                w, c0 = w_in, COL[a]
            elif kind == "dv":
                pair, half = a
                c0 = COL["dv"] + 2 * P * pair
                return w_in[0].rearrange("(k p) n -> p k n", p=P)[:, 4 * half:4 * half + 4, c0:c0 + 2 * P]
            elif kind == "q":
                w, c0 = w_in, COL["nq"] + P * a
            else:
                w, c0 = w_in, COL[kind] + P * a
            return w[0].rearrange("(k p) n -> p k n", p=P)[:, :, c0:c0 + P]

        def chunk_cols(k):
            return SLOT if chunks[k][0] == "vg" else 1024

        turns = [[(kt, ps[2 + kt % 4]) for kt in range(KT)],
                 [(kt, ps[2 + i % 4]) for i, kt in enumerate(MIX_ORDER)],
                 [(kt, (ps[0], ps[1], ps[6], ps[7], ps[2], ps[3], ps[4], ps[5])[kt]) for kt in range(KT)]]

        block = ctx.enter_context(nc.Block())

        @block.sync
        def _(sp):
            for t in range(NT):
                sp.dma_start(xres[:, t, :], x[0, t * P:(t + 1) * P, :]).then_inc(s_x[t], 16)
            for n, (what, a) in enumerate(raws):
                if n >= RAW_SLOTS:
                    was, b = raws[n - RAW_SLOTS]
                    if was == "chunk":
                        sp.wait_ge(s_split, b + 1)
                    else:
                        sp.wait_ge(s_w1, w1_order.index(b) + 1)
                dst = raw[:, n % RAW_SLOTS, :]
                signal = s_raw[n % RAW_SLOTS]
                if what == "w1":
                    kv, j = a
                    src = (cmp_w1_k, cmp_w1_v)[kv][0].rearrange("(j p) n -> p j n", p=P)[:, 4 * j:4 * j + 4, :]
                    sp.dma_start(dst[:, 0:1024].rearrange("p (k n) -> p k n", k=4), src).then_inc(signal, 16)
                elif chunks[a][0] == "vg":
                    half = chunks[a][1]
                    w = w_in[0].rearrange("(k p) n -> p k n", p=P)[:, 4 * half:4 * half + 4, :]
                    dst = dst.rearrange("p (k n) -> p k n", k=4)
                    sp.dma_start(dst[:, :, 0:P], w[:, :, COL["vsl"]:COL["vsl"] + P]).then_inc(signal, 16)
                    sp.dma_start(dst[:, :, P:V_COLS], w[:, :, COL["vw"]:COL["gt"] + GATES]).then_inc(signal, 16)
                else:
                    src = chunk_src(a)
                    sp.dma_start(dst[:, 0:1024].rearrange("p (k n) -> p k n", k=src.shape[1]), src).then_inc(signal, 16)
            for t in range(NT - 1):
                sp.wait_ge(s_y, t + 1)
                sp.dma_start(out[0, t * P:(t + 1) * P, :], xres[:, t, :]).then_inc(s_out, 16)
            sp.wait_ge(s_out, 16 * NT)

        def raw_landed(eng, item):
            n = raw_of[item]
            loads = sum(2 if raws[m][0] == "chunk" and chunks[raws[m][1]][0] == "vg" else 1
                        for m in range(n % RAW_SLOTS, n + 1, RAW_SLOTS))
            eng.wait_ge(s_raw[n % RAW_SLOTS], 16 * loads)

        @block.gpsimd
        def _(pool):
            pool.dma_start(ident[:, :], c_ident).then_inc(s_ident, 16)
            pool.dma_start(rows[0:8, :], norm1[0].rearrange("(k p) -> k p", p=P)).then_inc(s_rows, 16)
            pool.dma_start(rows[8:16, :], norm2[0].rearrange("(k p) -> k p", p=P)).then_inc(s_rows, 16)
            pool.dma_start(rows[16:17, :], diff_subln).then_inc(s_rows, 16)
            pool.dma_start(rows[17:21, :], nsa_norm[0].rearrange("(k p) -> k p", p=P)).then_inc(s_rows, 16)
            pool.dma_start(rows[21:37, :], cmp_pos_k[0].rearrange("(j l) d -> j (l d)", l=2)).then_inc(s_rows, 16)
            pool.dma_start(rows[37:53, :], cmp_pos_v[0].rearrange("(j l) d -> j (l d)", l=2)).then_inc(s_rows, 16)
            pool.dma_start(relb[:, :], rel_bias).then_inc(s_btab, 16)
            pool.dma_start(choice[:, :], c_choice).then_inc(s_btab, 16)
            pool.dma_start(causal[:, :], c_causal).then_inc(s_btab, 16)
            for n, v in enumerate((lambda_q1, lambda_k1, lambda_q2, lambda_k2)):
                pool.dma_start(lam_in[:, n, :], v[0].partition_broadcast(P)).then_inc(s_lamin, 16)
            for n, v in enumerate((cmp_w2_k, cmp_w2_v)):
                pool.dma_start(w2[:, n, :, :], v[0].rearrange("(m p) d -> p m d", p=P)).then_inc(s_small, 16)
            pool.dma_start(cmask[:, :, :], c_cmask).then_inc(s_small, 16)
            pool.dma_start(has_cmp[:, :], c_has).then_inc(s_small, 16)
            for k in range(len(chunks)):
                n = chunk_cols(k)
                pool.wait_ge(s_whi, k + 1)
                nc.gpsimd.tensor_tensor(wv_lo(k)[:, 0:n], raw[:, raw_of[("chunk", k)] % RAW_SLOTS, 0:n],
                                        wv_hi(k)[:, 0:n].bitcast(F32), ALU.subtract).then_inc(s_split, 1)
            pool.wait_ge(s_final_g, 16)
            for t in range(NT):
                pool.wait_ge(s_ss, 18 + t + 1)
                z = xres[:, t, 512:1024]
                nc.gpsimd.tensor_tensor(z, z, final_g[:, 512:1024], ALU.mult).then_inc(s_gx, 1)

        @block.tensor
        def _(pe):
            def three(o, a_hi, a_lo, b_hi, b_lo, first, last):
                nc.tensor.matmul(o, a_hi, b_hi, start=first, stop=False)
                nc.tensor.matmul(o, a_hi, b_lo, start=False, stop=False)
                return nc.tensor.matmul(o, a_lo, b_hi, start=False, stop=last)

            def turn_tile(stage, i, src):
                kt, bank = turns[stage][i]
                if stage < 2 and i >= 4:
                    pe.wait_ge(s_tlo, stage * KT + i - 3)
                for t in range(NT):
                    mm = nc.tensor.transpose(bank[:, t * P:(t + 1) * P], src[:, t, kt * P:(kt + 1) * P], ident[:, :])
                mm.then_inc(s_tp, 1)

            def columns(bank, k, kt):
                hi, lo = wv_hi(k)[:, kt * P:(kt + 1) * P], wv_lo(k)[:, kt * P:(kt + 1) * P]
                nc.tensor.matmul(bank[:, :], hi, xT_hi[:, kt, :], start=kt == 0, stop=False)
                nc.tensor.matmul(bank[:, :], hi, xT_lo[:, kt, :], start=False, stop=False)
                return nc.tensor.matmul(bank[:, :], lo, xT_hi[:, kt, :], start=False, stop=kt == KT - 1)

            def proj_piece(k, piece):
                kind, a = chunks[k]
                if piece == 0:
                    pe.wait_ge(s_split, release(k) + 1)
                    if k >= 2:
                        pe.wait_ge(s_evac, k - 1)
                if kind in ("vg", "dv"):
                    half = a if kind == "vg" else a[1]
                    n = V_COLS if kind == "vg" else 2 * P
                    tt = piece // 4
                    t = 2 * half + tt
                    o = ps[2 + t][:, 0:n] if kind == "vg" else PROJ[k % 2][:, tt * n:(tt + 1) * n]
                    for kt in range(2 * (piece % 4), 2 * (piece % 4) + 2):
                        kw = k - half + kt // 4
                        c = (kt % 4) * n
                        mm = three(o, xT_hi[:, kt, t * P:(t + 1) * P], xT_lo[:, kt, t * P:(t + 1) * P],
                                   wv_hi(kw)[:, c:c + n], wv_lo(kw)[:, c:c + n], kt == 0, kt == KT - 1)
                else:
                    if k == 0:
                        pe.wait_ge(s_tlo, piece + 1)
                    mm = columns(PROJ[k % 2], k, piece)
                if piece == PIECES - 1:
                    mm.then_inc(s_chunk, 1)

            def proj_chunk(k):
                for piece in range(PIECES):
                    proj_piece(k, piece)

            def hidden(kv, j):
                if j == 0:
                    pe.wait_ge(s_evac, kv + 1)
                    pe.wait_ge(s_bvec, 1)
                raw_landed(pe, ("w1", (kv, j)))
                w = raw[:, raw_of[("w1", (kv, j))] % RAW_SLOTS, :]
                for jj in range(4):
                    mm = nc.tensor.matmul(OUTP[kv][0:GROUPS * NC, 0:CMP_HIDDEN],
                                          blk[kv][:, 4 * j + jj, :, :].rearrange("p g n -> p (g n)"),
                                          w[:, jj * CMP_HIDDEN:(jj + 1) * CMP_HIDDEN],
                                          start=(j == 0 and jj == 0), stop=(j == 3 and jj == 3))
                mm.then_inc(s_w1, 1)

            def hidden_turn(kv):
                pe.wait_ge(s_gelu, kv + 1)
                for m in range(2):
                    c = CMP_HIDDEN + m * GROUPS * NC
                    mm = nc.tensor.transpose(OUTP[kv][:, c:c + GROUPS * NC], hid_rows[:, kv, m * P:(m + 1) * P],
                                             ident[0:GROUPS * NC, 0:GROUPS * NC])
                mm.then_inc(s_hid_t, 1)

            def compressed():
                pe.wait_ge(s_small, 16 * 4)
                pe.wait_ge(s_hid_c, 1)
                for m in range(2):
                    mm = nc.tensor.matmul(ps[6][0:HD, 0:GROUPS * NC], w2[:, 0, m, :], hid[:, 0, m, :],
                                          start=m == 0, stop=m == 1)
                mm.then_inc(s_kvc, 1)
                pe.wait_ge(s_hid_c, 2)
                for g in range(GROUPS):
                    for m in range(2):
                        mm = nc.tensor.matmul(ps[7][0:NC, g * HD:(g + 1) * HD], hid[:, 1, m, g * NC:(g + 1) * NC],
                                              w2[:, 1, m, :], start=m == 0, stop=m == 1)
                mm.then_inc(s_kvc, 1)

            def scores(s):
                kind, h, b, i = slots[s]
                bank = SCORE[s % 2]
                pe.wait_ge(s_evac, needed(slots[s]))
                if s >= 2:
                    pe.wait_ge(s_exp, s - 1)
                if s == 0:
                    pe.wait_ge(s_cmp_ready, 1)
                if kind == "cmp":
                    for hh in range(NSA_HEADS):
                        q = q_nsa[:, hh, i * P:(i + 1) * P]
                        o = bank[:, hh * NC:(hh + 1) * NC]
                        nc.tensor.matmul(o, q, kc_s[:, 0, hh // HEADS_PER_GROUP, :], start=True, stop=False)
                        mm = nc.tensor.matmul(o, q, kc_s[:, 1, hh // HEADS_PER_GROUP, :], start=False, stop=True)
                else:
                    n = (i + 1) * P
                    if kind == "nsa":
                        q = q_nsa[:, h, i * P:(i + 1) * P]
                        k_hi = k_nsa[:, 0, 2 * b + h // HEADS_PER_GROUP, 0:n]
                        k_lo = k_nsa[:, 1, 2 * b + h // HEADS_PER_GROUP, 0:n]
                    else:
                        q = q_diff[:, h % 2, b, i * P:(i + 1) * P]
                        k_hi, k_lo = k_diff[:, h % 2, 0, b, 0:n], k_diff[:, h % 2, 1, b, 0:n]
                    nc.tensor.matmul(bank[:, 0:n], q, k_hi, start=True, stop=False)
                    mm = nc.tensor.matmul(bank[:, 0:n], q, k_lo, start=False, stop=True)
                mm.then_inc(s_qk, 1)

            def turn_probs(s):
                if s not in turn:
                    return
                kind, h, b, i = slots[s]
                n = turn[s]
                if kind == "diff":
                    pe.wait_ge(s_comb, sum(1 for z in turned[:n + 1] if slots[z][0] == "diff"))
                else:
                    pe.wait_ge(s_exp, s + 1)
                if n >= 2:
                    pe.wait_ge(s_pt, n - 1)
                for j in range(2 if kind == "cmp" else i + 1):
                    mm = nc.tensor.transpose(TURN[n % 2][:, j * P:(j + 1) * P], E[:, s % E_SLOTS, j * P:(j + 1) * P],
                                             ident[:, :])
                mm.then_inc(s_turn, 1)

            def values(s):
                if s not in turn:
                    return
                kind, h, b, i = slots[s]
                n = turn[s]
                bank = OUTP[n % 2]
                pe.wait_ge(s_pt, n + 1)
                if n >= 2:
                    pe.wait_ge(s_of, n - 1)
                if kind == "cmp":
                    for g in range(GROUPS):
                        mm = nc.tensor.matmul(bank[:, g * 256:(g + 1) * 256], PT[:, n % 2, g * P:(g + 1) * P],
                                              vc_bd[:, g, :], start=True, stop=True)
                else:
                    g = h // HEADS_PER_GROUP
                    for j in range(i + 1):
                        v = v_nsa[:, b, j, g * HD:(g + 1) * HD] if kind == "nsa" else v_diff[:, j, (h % 2) * P:(h % 2 + 1) * P]
                        mm = nc.tensor.matmul(bank[:, 0:v.shape[1]], PT[:, n % 2, j * P:(j + 1) * P], v,
                                              start=j == 0, stop=j == i)
                mm.then_inc(s_pv, 1)

            pe.wait_ge(s_ones, 1)
            for n in range(WARM):
                nc.tensor.matmul(ps[0][:, 0:P], ones[:, :], ones[:, :], start=True, stop=True)
            pe.wait_ge(s_ident, 16)
            pe.wait_ge(s_rows, 16 * 6)
            nc.tensor.transpose(ps[6][:, 0:N_ROWS], rows[0:N_ROWS, :], ident[0:N_ROWS, 0:N_ROWS]).then_inc(s_cols_t, 1)
            pe.wait_ge(s_btab, 16 * 3)
            nc.tensor.matmul(ps[7][0:NHEADS, 0:384], relb[:, :], choice[:, :], start=True, stop=True).then_inc(s_bvec_p, 1)

            pe.wait_ge(s_norm, NT)
            for i in range(KT):
                turn_tile(0, i, mix)
            for k in range(6):
                proj_chunk(k)
                for kv, j in w1_after.get(k, []):
                    hidden(kv, j)
            hidden_turn(0)
            for piece in range(PIECES):
                if piece == 4:
                    hidden_turn(1)
                proj_piece(6, piece)
            compressed()

            upto = 0
            while upto < LEAD_PIECES:
                proj_piece(n_base + upto // PIECES, upto % PIECES)
                upto += 1
            for s in range(n_slots + 4):
                if 3 <= s < n_slots + 3:
                    turn_probs(s - 3)
                if s < n_slots:
                    scores(s)
                    while upto < piece_upto[s]:
                        proj_piece(n_base + upto // PIECES, upto % PIECES)
                        upto += 1
                if s >= 4:
                    values(s - 4)

            def rows_chunk(k, a_hi, a_lo, banks, first, last, final=False):
                kc = chunks[k][1][1]
                pe.wait_ge(s_split, k + 1)
                order = [(kk, t) for t in range(NT) for kk in range(2)] if final else \
                        [(kk, t) for kk in range(2) for t in range(NT)]
                for kk, t in order:
                    hi, lo = wv_hi(k)[:, kk * 512:(kk + 1) * 512], wv_lo(k)[:, kk * 512:(kk + 1) * 512]
                    f = 2 * kc + kk
                    mm = three(banks[t][:, :], a_hi[:, f, t * P:(t + 1) * P], a_lo[:, f, t * P:(t + 1) * P],
                               hi, lo, first and kk == 0, last and kk == 1)
                    if final and kk == 1:
                        mm.then_inc(s_last, 1)
                if not final:
                    mm.then_inc(s_chunk, 1)

            pe.wait_ge(s_norm, 2 * NT)
            for i in range(6):
                turn_tile(1, i, mix)
            pe.wait_ge(s_of, len(turned))
            pe.wait_ge(s_evac, n_proj)
            for n, kc in enumerate(OUT_ORDER):
                if n == 2:
                    pe.wait_ge(s_norm, 3 * NT)
                    for i in (6, 7):
                        turn_tile(1, i, mix)
                pe.wait_ge(s_tlo, KT + 2 * n + 2)
                rows_chunk(index[("o", (0, kc))], mixT_hi, mixT_lo, FOUR[0], n == 0, n == 3)
            for n, kc in enumerate(OUT_ORDER):
                if n == 2:
                    pe.wait_ge(s_resid, NT)
                    for i in range(4):
                        turn_tile(2, i, xres)
                rows_chunk(index[("o", (1, kc))], mixT_hi, mixT_lo, FOUR[1], n == 0, n == 3)

            pe.wait_ge(s_tlo, 2 * KT + 4)
            pe.wait_ge(s_split, index[("up", 0)] + 1)
            for kt in range(4):
                columns(PROJ[0], index[("gate", 0)], kt)
            for kt in range(4):
                columns(OUTP[0], index[("up", 0)], kt)
            pe.wait_ge(s_resid, 2 * NT)
            for i in range(4, KT):
                turn_tile(2, i, xres)
            for kind, bank in (("gate", PROJ[0]), ("up", OUTP[0])):
                for kt in range(4, KT):
                    pe.wait_ge(s_tlo, 2 * KT + kt + 1)
                    mm = columns(bank, index[(kind, 0)], kt)
                mm.then_inc(s_chunk, 1)
            for f in range(1, FT):
                for kind, bank, read in (("gate", PROJ[f % 2], s_gn), ("up", OUTP[f % 2], s_un)):
                    k = index[(kind, f)]
                    pe.wait_ge(s_split, k + 1)
                    if f >= 2:
                        pe.wait_ge(read, f - 1)
                    for kt in range(KT):
                        mm = columns(bank, k, kt)
                    mm.then_inc(s_chunk, 1)
                    if k == index[("gate", 1)]:
                        pe.wait_ge(s_diag, 1)
                        nc.tensor.matmul(ps[2][:, :], ones[:, :], diag[:, :], start=True, stop=True).then_inc(s_nb_t, 1)
            for dh in range(2):
                for kc in range(FT // 2):
                    pe.wait_ge(s_alo, 2 * kc + 2 if dh == 0 else FT)
                    rows_chunk(index[("down", (dh, kc))], act_hi, act_lo, FOUR[1 - dh], kc == 0, kc == FT // 2 - 1,
                               final=(dh == 1 and kc == FT // 2 - 1))

        @block.scalar
        def _(act):
            def weights_hi(k):
                if k >= len(chunks):
                    return
                n = chunk_cols(k)
                raw_landed(act, ("chunk", k))
                if k >= SPLIT_SLOTS:
                    act.wait_ge(s_chunk, release(k - SPLIT_SLOTS) + 1)
                nc.scalar.copy(wv_hi(k)[:, 0:n], raw[:, raw_of[("chunk", k)] % RAW_SLOTS, 0:n]).then_inc(s_whi, 1)

            def square(src, junk, col, n):
                if n >= 2:
                    act.wait_ge(s_ss, n - 1)
                nc.scalar.activation(junk, src, ACT.Square, accum_out=stat[:, col:col + 1]).then_inc(s_ss, 1)

            def root(n, *ranges):
                act.wait_ge(s_root_in, n)
                for a, b in ranges:
                    ins = nc.scalar.activation(stat[:, 32 + a:32 + b], stat[:, a:b], ACT.Sqrt)
                ins.then_inc(s_root, 1)

            def split_hi(stage, i, gain):
                kt, bank = turns[stage][i]
                act.wait_ge(s_tp, stage * KT + i + 1)
                nc.scalar.activation((mixT_hi if stage == 1 else xT_hi)[:, kt, :], bank[:, :], ACT.Copy,
                                     scale=cols[:, gain:gain + 1]).then_inc(s_thi, 1)

            def evac_hi(k):
                kind, a = chunks[k]
                if kind not in ("q", "k", "dq", "dk"):
                    return
                act.wait_ge(s_chunk, k + 1)
                if kind in ("dq", "dk") and a >= 2:
                    act.wait_ge(s_qk, last_diff_qk[a - 2] + 1)
                if kind == "dq" and a < 2:
                    act.wait_ge(s_w1, 8)
                for hd in range(2):
                    src = PROJ[k % 2][hd * HD:(hd + 1) * HD, :]
                    if kind in ("q", "dq"):
                        dst = q_nsa[0:HD, 2 * a + hd, :] if kind == "q" else q_diff[0:HD, a % 2, hd, :]
                        ins = nc.scalar.activation(dst, src, ACT.Copy, scale=-SCALE)
                    else:
                        dst = (k_nsa[0:HD, 0, 2 * (a == "kw") + hd, :] if kind == "k"
                               else k_diff[0:HD, a % 2, 0, hd, :])
                        ins = nc.scalar.activation(dst, src, ACT.Copy)
                    ins.then_inc(s_hi, 1)

            def gelu(kv):
                act.wait_ge(s_w1, w1_order.index((kv, 3)) + 1)
                nc.scalar.activation(hid_rows[:, kv, :], OUTP[kv][0:GROUPS * NC, 0:CMP_HIDDEN],
                                     ACT.Gelu_apprx_tanh).then_inc(s_gelu, 1)

            def load_bias(n):
                h = bias_order[n]
                if n == 0:
                    act.wait_ge(s_spread, 16)
                if n >= BIAS_SLOTS:
                    act.wait_ge(s_add, bias_last[bias_order[n - BIAS_SLOTS]] + 1)
                base = bias_rows[h, 0, :]
                src = bass.AP(base.tensor, base.offset + 127, [[383, P], [1, 256]])
                act.dma_start(bias[:, n % BIAS_SLOTS, 256:512], src).then_inc(s_bias[n % BIAS_SLOTS], 16)

            def exps(s):
                kind, h, b, i = slots[s]
                n = 256 if kind == "cmp" else (i + 1) * P
                act.wait_ge(s_add, s + 1)
                if s >= E_SLOTS:
                    last = s - E_SLOTS
                    if last not in turn:
                        last += 1
                    act.wait_ge(s_turn, turns_upto[last])
                if kind == "cmp":
                    nc.scalar.activation(E[:, s % E_SLOTS, 0:n], SCORE[s % 2][:, 0:n], ACT.Exp, scale=-1.0).then_inc(s_exp, 1)
                else:
                    nc.scalar.activation(E[:, s % E_SLOTS, 0:n], SCORE[s % 2][:, 0:n], ACT.Exp, scale=-1.0,
                                         bias=nmax[:, s:s + 1], accum_out=ssum[:, s:s + 1]).then_inc(s_exp, 1)

            def copy_turned(s):
                if s not in turn:
                    return
                kind, h, b, i = slots[s]
                n = turn[s]
                w = 256 if kind == "cmp" else (i + 1) * P
                act.wait_ge(s_turn, n + 1)
                if n >= 2:
                    act.wait_ge(s_pv, n - 1)
                nc.scalar.copy(PT[:, n % 2, 0:w], TURN[n % 2][:, 0:w]).then_inc(s_pt, 1)

            act.wait_ge(s_zero, 1)
            nc.scalar.activation(stat[:, 63:64], stat[:, 62:63], ACT.Sqrt)
            for t in range(NT):
                if t % 2 == 0:
                    act.wait_ge(s_x[t], 16)
                    square(xres[:, t, :], E[:, t:t + 2, :].rearrange("p a b -> p (a b)"), 20 + t, t // 2)
                root(t + 1, (20 + t, 21 + t))
                if t == 1:
                    weights_hi(0)
            weights_hi(1)
            act.wait_ge(s_cols, 1)
            for i in range(KT):
                split_hi(0, i, C_N1 + i)
                if i == 3:
                    weights_hi(2)
            act.wait_ge(s_bvec, 1)
            act.dma_start(bias_scratch[:, :], bias_vec[:, :]).then_inc(s_scratch, 16)
            act.wait_ge(s_scratch, 16)
            act.dma_start(bias_rows[:, :, :], bias_scratch[:, :].unsqueeze(1).to_broadcast([NHEADS, P, 384])).then_inc(s_spread, 16)
            act.wait_ge(s_lamdot, 1)
            nc.scalar.activation(lam[:, 2:4], lam[:, 0:2], ACT.Exp).then_inc(s_lamexp, 1)
            load_bias(0)
            load_bias(1)
            weights_hi(3)
            evac_hi(2)
            weights_hi(4)
            weights_hi(5)
            act.wait_ge(s_evac, 5)
            nc.scalar.activation(gates[:, :, :], gates[:, :, :], ACT.Exp, scale=-1.0).then_inc(s_gexp, 1)
            gelu(0)
            evac_hi(5)
            weights_hi(6)
            gelu(1)
            for k in range(7, 10):
                weights_hi(k)
            evac_hi(6)
            weights_hi(10)
            act.wait_ge(s_kvc, 1)
            nc.scalar.copy(kc_s[0:HD, 0, :, :].rearrange("p g n -> p (g n)"), ps[6][0:HD, 0:GROUPS * NC]).then_inc(s_kchi, 1)

            for s in range(n_slots + 4):
                if 3 <= s < n_slots + 3:
                    copy_turned(s - 3)
                if s < n_slots:
                    for n in range(2, NHEADS):
                        if s == bias_first[bias_order[n - 1]]:
                            load_bias(n)
                    exps(s)
                    for k in chunks_done_in[s]:
                        evac_hi(k)
                        for j in (k - 1, k):
                            if release(j) == k:
                                weights_hi(j + SPLIT_SLOTS)
                    if s in (early - 1, early, early + 1, early + 2):
                        t = s - early + 1
                        act.wait_ge(s_of, turn[cmp_last - 3 + t] + 1)
                        square(mix[:, t, 512:1024], mixT_lo[:, t, :], 16 + t, 2 + t)
                    if s == early_norm:
                        root(5, (0, 8), (16, 20))
                if s == n_slots:
                    act.wait_ge(s_zero, 1)
                    nc.scalar.activation(stat[:, 63:64], stat[:, 62:63], ACT.Sqrt)

            root(6, (8, 16))
            for i, kt in enumerate(MIX_ORDER):
                split_hi(1, i, C_SUB if kt < 4 else C_NSA + kt - 4)
            o0 = index[("o", (0, OUT_ORDER[0]))]
            for n in range(4):
                weights_hi(o0 + n + 4)
            for t in range(NT):
                act.wait_ge(s_resid, t + 1)
                square(xres[:, t, 0:512], E[:, t % 2, :], 20 + t, 6 + t)
            for n in range(4, 6):
                weights_hi(o0 + n + 4)
            for i in range(4):
                split_hi(2, i, C_N2 + i)
            for n in range(6, 8):
                weights_hi(o0 + n + 4)
            for i in range(4, KT):
                split_hi(2, i, C_N2 + i)
            for t in range(NT):
                act.wait_ge(s_resid, NT + t + 1)
                square(xres[:, t, 512:1024], E[:, t % 2, :], 24 + t, 10 + t)
            root(7, (20, 24))
            act.wait_ge(s_nb_t, 1)
            nc.scalar.copy(norm_b[:, :], ps[2][:, :]).then_inc(s_nb, 1)
            act.dma_start(final_g[:, :], final_norm.partition_broadcast(P)).then_inc(s_final_g, 16)
            for f in range(FT):
                weights_hi(index[("gate", f)] + SPLIT_SLOTS)
                act.wait_ge(s_gn, f + 1)
                nc.scalar.activation(gate_n[:, f % 2, :], gate_n[:, f % 2, :], ACT.Silu).then_inc(s_silu, 1)
                weights_hi(index[("up", f)] + SPLIT_SLOTS)
                act.wait_ge(s_prod, f + 1)
                nc.scalar.copy(act_hi[:, f, :], up_n[:, f % 2, :]).then_inc(s_ahi, 1)
            for kc in range(FT // 2):
                weights_hi(index[("down", (0, kc))] + SPLIT_SLOTS)
            for t in range(NT):
                act.wait_ge(s_resid, 2 * NT + t + 1)
                square(xres[:, t, 0:512], gate_n[:, t % 2, :], 20 + t, 14 + t)
            nc.scalar.activation(stat[:, 63:64], stat[:, 62:63], ACT.Sqrt)
            for kc in range(FT // 2 - SPLIT_SLOTS):
                weights_hi(index[("down", (1, kc))] + SPLIT_SLOTS)
            for t in range(NT):
                act.wait_ge(s_resid, 3 * NT + t + 1)
                square(xres[:, t, 512:1024], gate_n[:, t % 2, :], 24 + t, 18 + t)
            root(8, (20, 24))
            act.wait_ge(s_final, 1)
            act.wait_ge(s_gx, NT)
            nc.scalar.activation(xres[:, NT - 1, :], xres[:, NT - 1, :], ACT.Copy,
                                 scale=stat[:, 52 + NT - 1:52 + NT]).then_inc(s_ya, 1)
            act.wait_ge(s_ya, 1)
            act.dma_start(out[0, (NT - 1) * P:T, :], xres[:, NT - 1, :]).then_inc(s_out, 16)

        @block.vector
        def _(dve):
            chain = [0]

            def link(ins):
                chain[0] += 1
                ins.then_inc(s_dve, 1)
                dve.wait_ge(s_dve, chain[0])

            def mean_root(*ranges):
                for a, b, width in ranges:
                    ins = nc.vector.tensor_scalar(stat[:, a:b], stat[:, a:b], 1.0 / width, EPS, ALU.mult, ALU.add)
                ins.then_inc(s_root_in, 1)

            def inverse_root(n, *ranges):
                dve.wait_ge(s_root, n)
                for a, b in ranges:
                    ins = nc.vector.reciprocal(stat[:, 32 + a:32 + b], stat[:, 32 + a:32 + b])
                link(ins)

            def scale_diff(t, pair):
                m = mix[:, t, 2 * P * pair:2 * P * (pair + 1)].rearrange("p (h n) -> p h n", n=P)
                c = 32 + 8 * pair + t
                r = stat[:, c:c + 5:4]
                return nc.vector.tensor_tensor(m, m, r.unsqueeze(2).to_broadcast([P, 2, P]), ALU.mult)

            def split_lo(stage, i, gain):
                kt, bank = turns[stage][i]
                hi, lo = (mixT_hi, mixT_lo) if stage == 1 else (xT_hi, xT_lo)
                dve.wait_ge(s_thi, stage * KT + i + 1)
                nc.vector.scalar_tensor_tensor(out=lo[:, kt, :], in0=bank[:, :], scalar=cols[:, gain:gain + 1],
                                               in1=hi[:, kt, :].bitcast(F32),
                                               op0=ALU.mult, op1=ALU.subtract).then_inc(s_tlo, 1)

            def evac(k):
                kind, a = chunks[k]
                bank = PROJ[k % 2]
                dve.wait_ge(s_chunk, k + 1)
                if kind == "c":
                    for par in range(2):
                        for g in range(GROUPS):
                            src = bank[g * HD:(g + 1) * HD, :]
                            src = bass.AP(src.tensor, src.offset + par, [src.ap[0], [2, 16], [CMP_STRIDE, N_CMP]])
                            pos = cols[par * HD:(par + 1) * HD, C_POS + 16 * a:C_POS + 16 * a + 16]
                            ins = nc.vector.tensor_tensor(blk[a][par * HD:(par + 1) * HD, :, g, 0:N_CMP], src,
                                                          pos.unsqueeze(2).to_broadcast([HD, 16, N_CMP]), ALU.add)
                elif kind == "vg":
                    for t in (2 * a, 2 * a + 1):
                        nc.vector.tensor_copy(gates[:, t, :], ps[2 + t][:, 2 * P:V_COLS])
                        ins = nc.vector.tensor_copy(v_nsa[:, :, t, :], ps[2 + t][:, 0:2 * P].rearrange("p (b n) -> p b n", b=2))
                elif kind == "dv":
                    pair, half = a
                    if pair == 1:
                        dve.wait_ge(s_pv, turn[last_diff_qk[1]] + 1)
                    ins = nc.vector.tensor_copy(v_diff[:, 2 * half:2 * half + 2, :].rearrange("p t n -> p (t n)"), bank[:, :])
                else:
                    for hd in range(2):
                        src = bank[hd * HD:(hd + 1) * HD, :]
                        dve.wait_ge(s_hi, hi_upto[k] - 1 + hd)
                        if kind in ("q", "dq"):
                            q = q_nsa[:, 2 * a + hd, :] if kind == "q" else q_diff[:, a % 2, hd, :]
                            ins = nc.vector.scalar_tensor_tensor(out=q[HD:P, :], in0=src, scalar=-SCALE,
                                                                 in1=q[0:HD, :].bitcast(F32),
                                                                 op0=ALU.mult, op1=ALU.subtract)
                        else:
                            if kind == "k":
                                hi, lo = (k_nsa[:, z, 2 * (a == "kw") + hd, :] for z in range(2))
                            else:
                                hi, lo = (k_diff[:, a % 2, z, hd, :] for z in range(2))
                            link(nc.vector.tensor_tensor(lo[0:HD, :], src, hi[0:HD, :].bitcast(F32), ALU.subtract))
                            nc.vector.tensor_copy(hi[HD:P, :], hi[0:HD, :])
                            ins = nc.vector.tensor_copy(lo[HD:P, :], lo[0:HD, :])
                ins.then_inc(s_evac, 1)

            def add_bias(s):
                kind, h, b, i = slots[s]
                bank = SCORE[s % 2]
                dve.wait_ge(s_qk, s + 1)
                if kind == "cmp":
                    z = bank[:, 0:NSA_HEADS * NC].rearrange("p (h n) -> p h n", n=NC)
                    link(nc.vector.tensor_tensor(z, z, cmask[:, i, :].unsqueeze(1).to_broadcast([P, NSA_HEADS, NC]), ALU.add))
                    link(nc.vector.tensor_reduce(cstat[:, i, 0, :], z, AX.X, ALU.min))
                    nc.vector.tensor_tensor(z, z, cstat[:, i, 0, :].unsqueeze(2).to_broadcast([P, NSA_HEADS, NC]),
                                            ALU.subtract).then_inc(s_add, 1)
                    return
                n = (i + 1) * P
                m = bias_order.index(bias_head(slots[s]))
                dve.wait_ge(s_bias[m % BIAS_SLOTS], 16 * (m // BIAS_SLOTS + 1))
                nc.vector.tensor_tensor_reduce(out=bank[:, 0:n], in0=bank[:, 0:n],
                                               in1=bias[:, m % BIAS_SLOTS, 512 - n:512], scale=1.0, scalar=3.0e38,
                                               op0=ALU.add, op1=ALU.min, accum_out=nmax[:, s:s + 1]).then_inc(s_add, 1)

            def weigh(s):
                kind, h, b, i = slots[s]
                dve.wait_ge(s_exp, s + 1)
                if kind == "cmp":
                    z = E[:, s % E_SLOTS, 0:256].rearrange("p (h n) -> p h n", n=NC)
                    link(nc.vector.tensor_reduce(cstat[:, i, 1, :], z, AX.X, ALU.add))
                    link(nc.vector.reciprocal(cstat[:, i, 2, :], cstat[:, i, 1, :]))
                    g0 = gates[:, i, :].rearrange("p (h c) -> p h c", c=3)[:, :, 0]
                    link(nc.vector.scalar_tensor_tensor(out=cstat[:, i, 3, :], in0=g0, scalar=has_cmp[:, i:i + 1],
                                                        in1=cstat[:, i, 2, :], op0=ALU.mult, op1=ALU.mult))
                    return
                if kind == "diff" and b == 0:
                    return
                link(nc.vector.reciprocal(ssum[:, s:s + 1], ssum[:, s:s + 1]))
                if kind == "nsa":
                    c = 3 * h + 1 + b
                    nc.vector.tensor_tensor(coef[:, s:s + 1], ssum[:, s:s + 1], gates[:, i, c:c + 1], ALU.mult).then_inc(s_coefs, 1)
                elif b == 1:
                    n = (i + 1) * P
                    e0, e1 = E[:, (s - 1) % E_SLOTS, 0:n], E[:, s % E_SLOTS, 0:n]
                    link(nc.vector.scalar_tensor_tensor(out=coef[:, s:s + 1], in0=ssum[:, s - 1:s], scalar=lam[:, 6:7],
                                                        in1=ssum[:, s:s + 1], op0=ALU.mult, op1=ALU.mult))
                    nc.vector.scalar_tensor_tensor(out=e1, in0=e1, scalar=coef[:, s:s + 1], in1=e0,
                                                   op0=ALU.mult, op1=ALU.add).then_inc(s_comb, 1)
                    link(nc.vector.reciprocal(coef[:, s - 1:s], ssum[:, s - 1:s]))

            def gather(s):
                if s not in turn:
                    return
                kind, h, b, i = slots[s]
                n = turn[s]
                bank = OUTP[n % 2]
                dve.wait_ge(s_pv, n + 1)
                if kind == "nsa":
                    dve.wait_ge(s_coefs, sum(1 for z in turned[:n + 1] if slots[z][0] == "nsa"))
                    m = mix[:, i, 512 + h * HD:512 + (h + 1) * HD]
                    if b == 0:
                        nc.vector.tensor_scalar(m, bank[:, 0:HD], coef[:, s:s + 1], None, ALU.mult).then_inc(s_of, 1)
                    else:
                        dve.wait_ge(s_of, n)
                        nc.vector.scalar_tensor_tensor(out=m, in0=bank[:, 0:HD], scalar=coef[:, s:s + 1], in1=m,
                                                       op0=ALU.mult, op1=ALU.add).then_inc(s_of, 1)
                elif kind == "diff":
                    m = mix[:, i, h * P:(h + 1) * P]
                    nc.vector.tensor_scalar(m, bank[:, 0:P], coef[:, s - 1:s], None, ALU.mult).then_inc(s_of, 1)
                    dve.wait_ge(s_of, n + 1)
                    c = 4 * h + i
                    link(nc.vector.tensor_tensor_reduce(out=sq[:, 0:P], in0=m, in1=m, scale=1.0, scalar=0.0, op0=ALU.mult,
                                                        op1=ALU.add, accum_out=stat[:, c:c + 1]))
                else:
                    z = bank[:, :].rearrange("p (h n) -> p h n", n=HD)
                    link(nc.vector.tensor_tensor(sq[:, :].rearrange("p (h n) -> p h n", n=HD), z,
                                                 cstat[:, i, 3, :].unsqueeze(2).to_broadcast([P, NSA_HEADS, HD]), ALU.mult))
                    m = mix[:, i, 512:1024]
                    nc.vector.tensor_tensor(m, m, sq[:, :], ALU.add).then_inc(s_of, 1)
                    dve.wait_ge(s_of, n + 1)

            nc.vector.memset(stat[:, 60:64], 1.0).then_inc(s_zero, 1)
            nc.vector.memset(ones[:, :], 1.0).then_inc(s_ones, 1)
            nc.vector.memset(bias[:, :, 0:256], 0.0)
            nc.vector.memset(vc_bd[:, :, :], 0.0)
            for kv in range(2):
                nc.vector.memset(blk[kv][:, :, :, N_CMP:NC], 0.0)
            link(nc.vector.memset(sq[:, :], 0.0))
            for t in range(NT):
                if t % 2 == 0:
                    dve.wait_ge(s_ss, t // 2 + 1)
                else:
                    dve.wait_ge(s_x[t], 16)
                    link(nc.vector.tensor_tensor_reduce(out=mix[:, t, :], in0=xres[:, t, :], in1=xres[:, t, :], scale=1.0,
                                                        scalar=0.0, op0=ALU.mult, op1=ALU.add,
                                                        accum_out=stat[:, 20 + t:21 + t]))
                mean_root((20 + t, 21 + t, D))
                inverse_root(t + 1, (20 + t, 21 + t))
                nc.vector.tensor_scalar(mix[:, t, :], xres[:, t, :], stat[:, 52 + t:53 + t], None, ALU.mult).then_inc(s_norm, 1)
            dve.wait_ge(s_cols_t, 1)
            link(nc.vector.tensor_copy(cols[:, 0:N_ROWS], ps[6][:, 0:N_ROWS]))
            nc.vector.tensor_scalar(cols[:, C_SUB:C_SUB + 1], cols[:, C_SUB:C_SUB + 1], 1.0 - LAMBDA_INIT, None,
                                    ALU.mult).then_inc(s_cols, 1)
            dve.wait_ge(s_bvec_p, 1)
            nc.vector.tensor_tensor(bias_vec[:, :], ps[7][0:NHEADS, 0:384], causal[:, :], ALU.add).then_inc(s_bvec, 1)
            dve.wait_ge(s_cols, 1)
            for i in range(KT):
                split_lo(0, i, C_N1 + i)
            dve.wait_ge(s_lamin, 16 * 4)
            for n in range(2):
                ins = nc.vector.tensor_tensor_reduce(out=sq[:, n * HD:(n + 1) * HD], in0=lam_in[:, 2 * n, :],
                                                     in1=lam_in[:, 2 * n + 1, :], scale=1.0, scalar=0.0, op0=ALU.mult,
                                                     op1=ALU.add, accum_out=lam[:, n:n + 1])
            ins.then_inc(s_lamdot, 1)
            dve.wait_ge(s_lamexp, 1)
            link(nc.vector.tensor_tensor(lam[:, 5:6], lam[:, 3:4], lam[:, 2:3], ALU.subtract))
            link(nc.vector.tensor_scalar(lam[:, 6:7], lam[:, 5:6], -LAMBDA_INIT, None, ALU.add))
            for k in range(5):
                evac(k)
            dve.wait_ge(s_gexp, 1)
            link(nc.vector.tensor_scalar(gates[:, :, :], gates[:, :, :], 1.0, None, ALU.add))
            link(nc.vector.reciprocal(gates[:, :, :], gates[:, :, :]))
            evac(5)
            for kv in range(2):
                dve.wait_ge(s_hid_t, kv + 1)
                nc.vector.tensor_copy(hid[:, kv, :, :].rearrange("p m n -> p (m n)"),
                                      OUTP[kv][:, CMP_HIDDEN:CMP_HIDDEN + 2 * GROUPS * NC]).then_inc(s_hid_c, 1)
            evac(6)
            dve.wait_ge(s_kchi, 1)
            k_hi, k_lo = (kc_s[:, z, :, :].rearrange("p g n -> p (g n)") for z in range(2))
            link(nc.vector.tensor_tensor(k_lo[0:HD, :], ps[6][0:HD, 0:GROUPS * NC], k_hi[0:HD, :].bitcast(F32), ALU.subtract))
            nc.vector.tensor_copy(k_hi[HD:P, :], k_hi[0:HD, :])
            nc.vector.tensor_copy(k_lo[HD:P, :], k_lo[0:HD, :])
            dve.wait_ge(s_kvc, 2)
            for g in range(GROUPS):
                for hh in range(HEADS_PER_GROUP):
                    ins = nc.vector.tensor_copy(vc_bd[hh * NC:(hh + 1) * NC, g, hh * HD:(hh + 1) * HD],
                                                ps[7][0:NC, g * HD:(g + 1) * HD])
            ins.then_inc(s_cmp_ready, 1)

            for s in range(n_slots + 4):
                if s < n_slots:
                    add_bias(s)
                if 1 <= s < n_slots + 1:
                    weigh(s - 1)
                if s < n_slots:
                    for k in chunks_done_in[s]:
                        evac(k)
                if s >= 4:
                    gather(s - 4)
                if s == early + 3:
                    dve.wait_ge(s_ss, 6)
                    mean_root((0, 8, P), (16, 20, 512))
                if s == early + 4:
                    inverse_root(5, (0, 8), (16, 20))
                if early + 5 <= s < early + 9:
                    t = s - early - 5
                    scale_diff(t, 0)
                    m = mix[:, t, 512:1024]
                    nc.vector.tensor_scalar(m, m, stat[:, 48 + t:49 + t], None, ALU.mult).then_inc(s_norm, 1)

            mean_root((8, 16, P))
            split_lo(1, 0, C_NSA)
            split_lo(1, 1, C_NSA + 1)
            inverse_root(6, (8, 16))
            for t in range(NT):
                scale_diff(t, 1).then_inc(s_norm, 1)
            for i in range(2, KT):
                kt = MIX_ORDER[i]
                split_lo(1, i, C_SUB if kt < 4 else C_NSA + kt - 4)

            def add_residual(t, dh, banks):
                z = xres[:, t, dh * 512:(dh + 1) * 512]
                nc.vector.tensor_tensor(z, z, banks[t][:, :], ALU.add).then_inc(s_resid, 1)

            def sum_halves():
                link(nc.vector.tensor_tensor(stat[:, 20:24], stat[:, 20:24], stat[:, 24:28], ALU.add))

            for dh in range(2):
                dve.wait_ge(s_chunk, index[("o", (dh, OUT_ORDER[3]))] + 1)
                for t in range(NT):
                    add_residual(t, dh, FOUR[dh])
                for i in range(4 * dh, 4 * dh + 4):
                    split_lo(2, i, C_N2 + i)
            dve.wait_ge(s_ss, 14)
            sum_halves()
            mean_root((20, 24, D))
            inverse_root(7, (20, 24))
            for t in range(NT):
                ins = nc.vector.tensor_scalar(diag[:, t * P:(t + 1) * P], ident[:, :], stat[:, 52 + t:53 + t], None, ALU.mult)
            ins.then_inc(s_diag, 1)
            dve.wait_ge(s_nb, 1)
            for f in range(FT):
                dve.wait_ge(s_chunk, index[("gate", f)] + 1)
                if f >= 2:
                    dve.wait_ge(s_prod, f - 1)
                nc.vector.tensor_tensor(gate_n[:, f % 2, :], PROJ[f % 2][:, :], norm_b[:, :], ALU.mult).then_inc(s_gn, 1)
                dve.wait_ge(s_chunk, index[("up", f)] + 1)
                if f >= 2:
                    dve.wait_ge(s_alo, f - 1)
                    dve.wait_ge(s_ahi, f - 1)
                nc.vector.tensor_tensor(up_n[:, f % 2, :], OUTP[f % 2][:, :], norm_b[:, :], ALU.mult).then_inc(s_un, 1)
                dve.wait_ge(s_un, f + 1)
                dve.wait_ge(s_silu, f + 1)
                nc.vector.tensor_tensor(up_n[:, f % 2, :], gate_n[:, f % 2, :], up_n[:, f % 2, :], ALU.mult).then_inc(s_prod, 1)
                dve.wait_ge(s_ahi, f + 1)
                nc.vector.tensor_tensor(act_lo[:, f, :], up_n[:, f % 2, :], act_hi[:, f, :].bitcast(F32),
                                        ALU.subtract).then_inc(s_alo, 1)
            dve.wait_ge(s_chunk, index[("down", (0, FT // 2 - 1))] + 1)
            for t in range(NT):
                add_residual(t, 0, FOUR[1])
            dve.wait_ge(s_final_g, 16)
            for t in range(NT):
                dve.wait_ge(s_ss, 14 + t + 1)
                z = xres[:, t, 0:512]
                ins = nc.vector.tensor_tensor(z, z, final_g[:, 0:512], ALU.mult)
            link(ins)
            for t in range(NT):
                dve.wait_ge(s_last, t + 1)
                add_residual(t, 1, FOUR[0])
            dve.wait_ge(s_ss, 22)
            sum_halves()
            mean_root((20, 24, D))
            dve.wait_ge(s_root, 8)
            nc.vector.reciprocal(stat[:, 52:56], stat[:, 52:56]).then_inc(s_final, 1)
            dve.wait_ge(s_final, 1)
            for t in range(NT - 1):
                dve.wait_ge(s_gx, t + 1)
                nc.vector.tensor_scalar(xres[:, t, :], xres[:, t, :], stat[:, 52 + t:53 + t], None, ALU.mult).then_inc(s_y, 1)


_INS = ["x", "norm1", "w_in", "lambda_q1", "lambda_k1", "lambda_q2", "lambda_k2", "diff_subln",
        "cmp_pos_k", "cmp_w1_k", "cmp_w2_k", "cmp_pos_v", "cmp_w1_v", "cmp_w2_v", "nsa_norm",
        "w_out", "norm2", "w_gate", "w_up", "w_down", "rel_bias", "final_norm"]


def kernel(**inputs):
    import concourse.bacc as _bacc
    from concourse.bass_utils import run_bass_kernel_spmd as _run

    nc = _bacc.Bacc("TRN2", target_bir_lowering=False, num_devices=1)
    arrays, args = {}, []
    for name in _INS:
        arrays[f"in_{name}_dram"] = np.ascontiguousarray(inputs[name])
    for name, a in shape_constants().items():
        arrays[f"in_{name}_dram"] = np.ascontiguousarray(a)
    for name, a in arrays.items():
        args.append(nc.dram_tensor(name, a.shape, mybir.dt.from_np(a.dtype), kind="ExternalInput").ap())
    args.append(nc.dram_tensor("bias_scratch", (NHEADS, 384), F32).ap())
    args.append(nc.dram_tensor("bias_rows", (NHEADS, P, 384), F32).ap())
    args.append(nc.dram_tensor("out_0_dram", (1, T, D), F32, kind="ExternalOutput").ap())
    hymba_block(nc, *args)
    r = _run(nc, [arrays], core_ids=[0])
    return r.results[0]["out_0_dram"]
```

```python
import math
from contextlib import ExitStack

import numpy as np

import concourse.bass as bass
from concourse import mybir

F32 = mybir.dt.float32
F32R = mybir.dt.float32r
ALU = mybir.AluOpType
ACT = mybir.ActivationFunctionType
AX = mybir.AxisListType

P = 128
D = 1024
T = 512
NT = T // P
KT = D // P
DIFF_HEADS, HD = 4, 64
NSA_HEADS, GROUPS = 8, 2
HEADS_PER_GROUP = NSA_HEADS // GROUPS
NHEADS = DIFF_HEADS + NSA_HEADS
N_BUCKETS, MAX_DISTANCE = 32, 128
CMP_LEN, CMP_STRIDE, CMP_HIDDEN = 32, 16, 256
N_CMP = (T - CMP_LEN) // CMP_STRIDE + 1
NC = 32
D_FF = 2816
FT = D_FF // P
EPS = 1e-6
NEG = 1e30
SCALE = HD ** -0.5
LAMBDA_INIT = 0.8 - 0.6 * math.exp(0.0)
COL = {"dq": 0, "dk": 512, "dv": 1024, "nq": 1536, "kc": 2048, "vc": 2176, "ksl": 2304, "vsl": 2432,
       "kw": 2560, "vw": 2688, "gt": 2816}
GATES = 24

WARM = 16
RAW_SLOTS = 3
SPLIT_SLOTS = 4
E_SLOTS = 4
BIAS_SLOTS = 3
PIECES = 8
PIECES_PER_SLOT = 1.35
LEAD_PIECES = 6
FILL_RATE = 2.5
V_COLS = 2 * P + GATES
SLOT = 4 * V_COLS
MIX_ORDER = (4, 5, 6, 7, 0, 1, 2, 3)


def shape_constants():
    ident = np.eye(P, dtype=np.float32)
    dist = 255 - np.arange(384)
    half = N_BUCKETS // 2
    pos = np.maximum(dist, 1).astype(np.float32)
    far = half + (np.log(pos / half) / math.log(MAX_DISTANCE / half) * (N_BUCKETS - half)).astype(np.int32)
    bucket = np.where(dist < half, np.maximum(dist, 0), np.minimum(far, N_BUCKETS - 1))
    choice = np.zeros((N_BUCKETS, 384), np.float32)
    for j in range(384):
        if dist[j] >= 0:
            choice[bucket[j], j] -= 1.0
            choice[N_BUCKETS - 1, j] += 1.0
    causal = np.broadcast_to(np.where(dist < 0, np.float32(NEG), np.float32(0)), (NHEADS, 384))
    q = np.arange(T)[:, None]
    n = np.arange(NC)[None, :]
    hidden = (n * CMP_STRIDE + CMP_LEN - 1 > q) | (n >= N_CMP)
    cmask = np.where(hidden, np.float32(NEG), np.float32(0)).reshape(NT, P, NC).transpose(1, 0, 2)
    has = (np.arange(T) >= CMP_LEN - 1).astype(np.float32).reshape(NT, P).T
    return {"c_ident": ident, "c_choice": choice, "c_causal": np.ascontiguousarray(causal),
            "c_cmask": np.ascontiguousarray(cmask), "c_has": np.ascontiguousarray(has)}


def plan_chunks():
    chunks = [("c", 0), ("c", 1), ("k", "ksl"), ("vg", 0), ("vg", 1), ("k", "kw"), ("q", 0)]
    base = len(chunks)
    chunks += [("q", 1), ("dq", 0), ("dk", 0), ("dv", (0, 0)), ("dv", (0, 1)), ("q", 2), ("dq", 1), ("dk", 1),
               ("q", 3), ("dq", 2), ("dk", 2), ("dv", (1, 0)), ("dv", (1, 1)), ("dq", 3), ("dk", 3)]
    proj = len(chunks)
    chunks += [("o", (dh, kc)) for kc2 in (2, 0) for dh in range(2) for kc in (kc2, kc2 + 1)]
    for f in range(FT):
        chunks += [("gate", f), ("up", f)]
    chunks += [("down", (dh, kc)) for dh in range(2) for kc in range(FT // 2)]
    return chunks, base, proj


def plan_slots():
    slots = []

    def nsa(pair):
        for h in (2 * pair, 2 * pair + 1):
            for b in range(2):
                slots.extend(("nsa", h, b, i) for i in range(NT))

    def diff(h):
        slots.extend(("diff", h, m, i) for i in range(NT) for m in range(2))

    nsa(0), nsa(1), diff(0), nsa(2), diff(1), nsa(3)
    last = slots[-NT:]
    del slots[-NT:]
    for t in range(NT):
        slots.extend((last[t], ("cmp", 0, 0, t)))
    diff(2), diff(3)
    return slots


def hymba_block(nc, x, norm1, w_in, lambda_q1, lambda_k1, lambda_q2, lambda_k2, diff_subln,
                cmp_pos_k, cmp_w1_k, cmp_w2_k, cmp_pos_v, cmp_w1_v, cmp_w2_v, nsa_norm,
                w_out, norm2, w_gate, w_up, w_down, rel_bias, final_norm,
                c_ident, c_choice, c_causal, c_cmask, c_has, bias_scratch, bias_rows, out):
    chunks, n_base, n_proj = plan_chunks()
    slots = plan_slots()
    n_slots = len(slots)
    index = {c: k for k, c in enumerate(chunks)}

    w1_after = {2: [(0, 0)], 3: [(1, 0), (0, 1)], 4: [(1, 1), (0, 2)], 5: [(1, 2), (0, 3)], 6: [(1, 3)]}
    raws = []
    for k, c in enumerate(chunks):
        raws.append(("chunk", k))
        if c == ("vg", 0):
            continue
        raws += [("w1", a) for a in (w1_after[k - 1] if c == ("vg", 1) else []) + w1_after.get(k, [])]
    raw_of = {r: n for n, r in enumerate(raws)}
    w1_order = [r[1] for r in raws if r[0] == "w1"]

    def needed(slot):
        kind, h, _, _ = slot
        if kind == "diff":
            return index[("dk", h)] + 1 if h else index[("dv", (0, 1))] + 1
        return index[("q", 3 if kind == "cmp" else h // 2)] + 1

    cmp_slot = [i for i, x_ in enumerate(slots) if x_[0] == "cmp"]
    cmp_last = cmp_slot[-1]
    early = cmp_last + 5
    n_fill = n_proj + 4
    n_pieces, all_pieces = (n_proj - n_base) * PIECES, (n_fill - n_base) * PIECES
    piece_upto, done = [], 0
    for s in range(n_slots + 4):
        ahead = min(s + 2, n_slots - 1)
        done = max(done, min(n_pieces, LEAD_PIECES + int(PIECES_PER_SLOT * (s + 1))), (needed(slots[ahead]) - n_base) * PIECES)
        if s >= early - 2:
            done = n_pieces
        if s >= early + 2:
            done = min(all_pieces, n_pieces + int(FILL_RATE * (s - early - 1)))
        piece_upto.append(done if s < n_slots + 3 else all_pieces)
    chunks_done_in = [[] for _ in range(n_slots + 4)]
    for k in range(n_base, n_fill):
        s = next(s for s in range(n_slots + 4) if piece_upto[s] >= (k - n_base + 1) * PIECES)
        chunks_done_in[s].append(k)
    groups_done_in = [[] for _ in range(n_slots + 4)]
    for g in range(2 * NT):
        s = next(s for s in range(n_slots + 4) if piece_upto[s] >= n_pieces + 4 * (g + 1))
        groups_done_in[s].append(g)

    turned = [s for s in range(n_slots) if not (slots[s][0] == "diff" and slots[s][2] == 0)]
    turn = {s: n for n, s in enumerate(turned)}
    turns_upto = [sum(1 for x_ in turned if x_ <= s) for s in range(n_slots)]

    def release(k):
        kind, a = chunks[k]
        pair = (kind == "vg" and a == 0) or (kind == "dv" and a[1] == 0) or (kind == "o" and a[1] == 2)
        return k + 1 if pair else k

    def bias_head(slot):
        return slot[1] if slot[0] == "diff" else DIFF_HEADS + slot[1]

    bias_order = []
    for s in slots:
        if s[0] != "cmp" and bias_head(s) not in bias_order:
            bias_order.append(bias_head(s))
    bias_first = {h: min(i for i, s in enumerate(slots) if s[0] != "cmp" and bias_head(s) == h) for h in bias_order}
    bias_last = {h: max(i for i, s in enumerate(slots) if s[0] != "cmp" and bias_head(s) == h) for h in bias_order}
    last_diff_qk = {h: max(i for i, s in enumerate(slots) if s[0] == "diff" and s[1] == h) for h in range(DIFF_HEADS)}

    hi_upto, n_hi = [], 0
    for c in chunks[:n_proj]:
        if c[0] in ("q", "k", "dq", "dk"):
            n_hi += 2
        hi_upto.append(n_hi)

    with ExitStack() as ctx:
        def sem(name):
            return ctx.enter_context(nc.semaphore(name))

        def sb(name, shape, dt=F32, stack=ctx):
            return stack.enter_context(nc.sbuf_tensor(name, shape, dt))

        ps = [ctx.enter_context(nc.psum_tensor(f"bank{b}", [P, 512], F32)) for b in range(8)]
        PROJ, SCORE, TURN, OUTP = ps[0:2], ps[2:4], ps[4:6], ps[6:8]
        FOUR = [[ps[0], ps[1], ps[6], ps[7]], [ps[2], ps[3], ps[4], ps[5]]]

        ident = sb("ident", [P, P])
        rows = sb("rows", [P, P])
        cols = sb("cols", [P, 56])
        relb = sb("relb", [N_BUCKETS, NHEADS])
        cmask = sb("cmask", [P, NT, NC])
        has_cmp = sb("has_cmp", [P, NT])
        lam = sb("lam", [P, 8])
        w2 = sb("w2", [P, 2, 2, HD])
        stat = sb("stat", [P, 64])
        gates = sb("gates", [P, NT, GATES])
        ones = sb("ones", [P, P])
        nmax = sb("nmax", [P, n_slots])
        ssum = sb("ssum", [P, n_slots])
        coef = sb("coef", [P, n_slots])
        cstat = sb("cstat", [P, NT, 4, NSA_HEADS])
        sq = sb("sq", [P, 512])
        xres = sb("xres", [P, NT, D])
        xT_hi = sb("xT_hi", [P, KT, T], F32R)
        xT_lo = sb("xT_lo", [P, KT, T], F32R)
        raw = sb("raw", [P, RAW_SLOTS, SLOT])
        w_hi = sb("w_hi", [P, SPLIT_SLOTS, SLOT], F32R)
        w_lo = sb("w_lo", [P, SPLIT_SLOTS, SLOT], F32R)

        with ExitStack() as attention:
            mix = sb("mix", [P, NT, D], F32, attention)
            with ExitStack() as mixed:
                mixT_hi = sb("mixT_hi", [P, KT, T], F32R, mixed)
                mixT_lo = sb("mixT_lo", [P, KT, T], F32R, mixed)
            q_nsa = sb("q_nsa", [P, NSA_HEADS, T], F32R, attention)
            k_nsa = sb("k_nsa", [P, 2, 2 * GROUPS, T], F32R, attention)
            v_nsa = sb("v_nsa", [P, 2, NT, P], F32, attention)
            v_diff = sb("v_diff", [P, NT, 2 * P], F32, attention)
            bias = sb("bias", [P, BIAS_SLOTS, 512], F32, attention)
            E = sb("E", [P, E_SLOTS, 512], F32, attention)
            PT = sb("PT", [P, 2, 512], F32, attention)
            kc_s = sb("kc_s", [P, 2, GROUPS, NC], F32R, attention)
            vc_bd = sb("vc_bd", [P, GROUPS, 4 * HD], F32, attention)
            hid = sb("hid", [P, 2, 2, GROUPS * NC], F32, attention)
            hid_rows = sb("hid_rows", [GROUPS * NC, 2, CMP_HIDDEN], F32, attention)
            with ExitStack() as compress:
                blk = [sb(f"blk{i}", [P, 16, GROUPS, NC], F32, compress) for i in range(2)]
                choice = sb("choice", [N_BUCKETS, 384], F32, compress)
                causal = sb("causal", [NHEADS, 384], F32, compress)
                bias_vec = sb("bias_vec", [NHEADS, 384], F32, compress)
                lam_in = sb("lam_in", [P, 4, HD], F32, compress)
            q_diff = sb("q_diff", [P, 2, 2, T], F32R, attention)
            k_diff = sb("k_diff", [P, 2, 2, 2, T], F32R, attention)
        with ExitStack() as swiglu:
            act_hi = sb("act_hi", [P, FT, T], F32R, swiglu)
            act_lo = sb("act_lo", [P, FT, T], F32R, swiglu)
            final_g = sb("final_g", [P, D], F32, swiglu)
            norm_b = sb("norm_b", [P, T], F32, swiglu)
            diag = sb("diag", [P, T], F32, swiglu)
            gate_n = sb("gate_n", [P, 2, T], F32, swiglu)
            up_n = sb("up_n", [P, 2, T], F32, swiglu)

        s_x = [sem(f"s_x{t}") for t in range(NT)]
        s_ident, s_rows, s_btab, s_small, s_lamin = sem("s_ident"), sem("s_rows"), sem("s_btab"), sem("s_small"), sem("s_lamin")
        s_final_g = sem("s_final_g")
        s_raw = [sem(f"s_raw{i}") for i in range(RAW_SLOTS)]
        s_bias = [sem(f"s_bias{i}") for i in range(BIAS_SLOTS)]
        s_scratch, s_spread = sem("s_scratch"), sem("s_spread")
        s_whi, s_split = sem("s_whi"), sem("s_split")
        s_chunk = sem("s_chunk")
        s_w1 = sem("s_w1")
        s_cols_t, s_cols = sem("s_cols_t"), sem("s_cols")
        s_bvec_p, s_bvec = sem("s_bvec_p"), sem("s_bvec")
        s_ss, s_root_in, s_root, s_norm = sem("s_ss"), sem("s_root_in"), sem("s_root"), sem("s_norm")
        s_tp, s_thi, s_tlo = sem("s_tp"), sem("s_thi"), sem("s_tlo")
        s_hi, s_evac = sem("s_hi"), sem("s_evac")
        s_gexp = sem("s_gexp")
        s_lamdot, s_lamexp = sem("s_lamdot"), sem("s_lamexp")
        s_gelu, s_hid_t, s_hid_c = sem("s_gelu"), sem("s_hid_t"), sem("s_hid_c")
        s_kvc, s_kchi, s_cmp_ready = sem("s_kvc"), sem("s_kchi"), sem("s_cmp_ready")
        s_zero, s_ones = sem("s_zero"), sem("s_ones")
        s_qk, s_add, s_exp, s_comb = sem("s_qk"), sem("s_add"), sem("s_exp"), sem("s_comb")
        s_turn, s_pt, s_pv, s_of = sem("s_turn"), sem("s_pt"), sem("s_pv"), sem("s_of")
        s_fill, s_filled = sem("s_fill"), sem("s_filled")
        s_coefs, s_resid = sem("s_coefs"), sem("s_resid")
        s_gn, s_un, s_diag, s_nb_t, s_nb = sem("s_gn"), sem("s_un"), sem("s_diag"), sem("s_nb_t"), sem("s_nb")
        s_last, s_gx = sem("s_last"), sem("s_gx")
        s_silu, s_prod, s_ahi, s_alo = sem("s_silu"), sem("s_prod"), sem("s_ahi"), sem("s_alo")
        s_y, s_ya, s_final, s_out = sem("s_y"), sem("s_ya"), sem("s_final"), sem("s_out")
        s_dve = sem("s_dve")

        C_N1, C_N2, C_SUB, C_NSA, C_POS = 0, 8, 16, 17, 21
        N_ROWS = 53

        def wv_hi(k):
            return w_hi[:, k % SPLIT_SLOTS, :]

        def wv_lo(k):
            return w_lo[:, k % SPLIT_SLOTS, :]

        def chunk_src(k):
            kind, a = chunks[k]
            if kind in ("o", "down"):
                w = w_out if kind == "o" else w_down
                dh, kc = a
                return w[0].rearrange("(k p) n -> p k n", p=P)[:, 2 * kc:2 * kc + 2, 512 * dh:512 * dh + 512]
            if kind in ("gate", "up"):
                w, c0 = (w_gate if kind == "gate" else w_up), P * a
            elif kind == "c":
                w, c0 = w_in, COL["kc" if a == 0 else "vc"]
            elif kind == "k":
                w, c0 = w_in, COL[a]
            elif kind == "dv":
                pair, half = a
                c0 = COL["dv"] + 2 * P * pair
                return w_in[0].rearrange("(k p) n -> p k n", p=P)[:, 4 * half:4 * half + 4, c0:c0 + 2 * P]
            elif kind == "q":
                w, c0 = w_in, COL["nq"] + P * a
            else:
                w, c0 = w_in, COL[kind] + P * a
            return w[0].rearrange("(k p) n -> p k n", p=P)[:, :, c0:c0 + P]

        def chunk_cols(k):
            return SLOT if chunks[k][0] == "vg" else 1024

        turns = [[(kt, ps[2 + kt % 4]) for kt in range(KT)],
                 [(kt, ps[i % 2] if i < 4 else ps[2 + i % 4]) for i, kt in enumerate(MIX_ORDER)],
                 [(kt, (ps[0], ps[1], ps[6], ps[7], ps[2], ps[3], ps[4], ps[5])[kt]) for kt in range(KT)]]

        block = ctx.enter_context(nc.Block())

        @block.sync
        def _(sp):
            for t in range(NT):
                sp.dma_start(xres[:, t, :], x[0, t * P:(t + 1) * P, :]).then_inc(s_x[t], 16)
            for n, (what, a) in enumerate(raws):
                if n >= RAW_SLOTS:
                    was, b = raws[n - RAW_SLOTS]
                    if was == "chunk":
                        sp.wait_ge(s_split, b + 1)
                    else:
                        sp.wait_ge(s_w1, w1_order.index(b) + 1)
                dst = raw[:, n % RAW_SLOTS, :]
                signal = s_raw[n % RAW_SLOTS]
                if what == "w1":
                    kv, j = a
                    src = (cmp_w1_k, cmp_w1_v)[kv][0].rearrange("(j p) n -> p j n", p=P)[:, 4 * j:4 * j + 4, :]
                    sp.dma_start(dst[:, 0:1024].rearrange("p (k n) -> p k n", k=4), src).then_inc(signal, 16)
                elif chunks[a][0] == "vg":
                    half = chunks[a][1]
                    w = w_in[0].rearrange("(k p) n -> p k n", p=P)[:, 4 * half:4 * half + 4, :]
                    dst = dst.rearrange("p (k n) -> p k n", k=4)
                    sp.dma_start(dst[:, :, 0:P], w[:, :, COL["vsl"]:COL["vsl"] + P]).then_inc(signal, 16)
                    sp.dma_start(dst[:, :, P:V_COLS], w[:, :, COL["vw"]:COL["gt"] + GATES]).then_inc(signal, 16)
                else:
                    src = chunk_src(a)
                    sp.dma_start(dst[:, 0:1024].rearrange("p (k n) -> p k n", k=src.shape[1]), src).then_inc(signal, 16)
            for t, by_act, by_dve in ((0, 0, 1), (1, 0, 2), (3, 1, 3), (2, 0, 4)):
                if by_act:
                    sp.wait_ge(s_ya, by_act)
                sp.wait_ge(s_y, by_dve)
                sp.dma_start(out[0, t * P:(t + 1) * P, :], xres[:, t, :]).then_inc(s_out, 16)
            sp.wait_ge(s_out, 16 * NT)

        def raw_landed(eng, item):
            n = raw_of[item]
            loads = sum(2 if raws[m][0] == "chunk" and chunks[raws[m][1]][0] == "vg" else 1
                        for m in range(n % RAW_SLOTS, n + 1, RAW_SLOTS))
            eng.wait_ge(s_raw[n % RAW_SLOTS], 16 * loads)

        @block.gpsimd
        def _(pool):
            pool.dma_start(ident[:, :], c_ident).then_inc(s_ident, 16)
            pool.dma_start(rows[0:8, :], norm1[0].rearrange("(k p) -> k p", p=P)).then_inc(s_rows, 16)
            pool.dma_start(rows[8:16, :], norm2[0].rearrange("(k p) -> k p", p=P)).then_inc(s_rows, 16)
            pool.dma_start(rows[16:17, :], diff_subln).then_inc(s_rows, 16)
            pool.dma_start(rows[17:21, :], nsa_norm[0].rearrange("(k p) -> k p", p=P)).then_inc(s_rows, 16)
            pool.dma_start(rows[21:37, :], cmp_pos_k[0].rearrange("(j l) d -> j (l d)", l=2)).then_inc(s_rows, 16)
            pool.dma_start(rows[37:53, :], cmp_pos_v[0].rearrange("(j l) d -> j (l d)", l=2)).then_inc(s_rows, 16)
            pool.dma_start(relb[:, :], rel_bias).then_inc(s_btab, 16)
            pool.dma_start(choice[:, :], c_choice).then_inc(s_btab, 16)
            pool.dma_start(causal[:, :], c_causal).then_inc(s_btab, 16)
            def split(k):
                n = chunk_cols(k)
                pool.wait_ge(s_whi, k + 1)
                nc.gpsimd.tensor_tensor(wv_lo(k)[:, 0:n], raw[:, raw_of[("chunk", k)] % RAW_SLOTS, 0:n],
                                        wv_hi(k)[:, 0:n].bitcast(F32), ALU.subtract).then_inc(s_split, 1)
            for k in range(2):
                split(k)
            for n, v in enumerate((lambda_q1, lambda_k1, lambda_q2, lambda_k2)):
                pool.dma_start(lam_in[:, n, :], v[0].partition_broadcast(P)).then_inc(s_lamin, 16)
            for n, v in enumerate((cmp_w2_k, cmp_w2_v)):
                pool.dma_start(w2[:, n, :, :], v[0].rearrange("(m p) d -> p m d", p=P)).then_inc(s_small, 16)
            pool.dma_start(cmask[:, :, :], c_cmask).then_inc(s_small, 16)
            pool.dma_start(has_cmp[:, :], c_has).then_inc(s_small, 16)
            for k in range(2, len(chunks)):
                split(k)
            pool.wait_ge(s_final_g, 16)
            for t in range(NT - 1):
                pool.wait_ge(s_ss, 18 + t + 1)
                z = xres[:, t, 512:1024]
                nc.gpsimd.tensor_tensor(z, z, final_g[:, 512:1024], ALU.mult).then_inc(s_gx, 1)

        @block.tensor
        def _(pe):
            def three(o, a_hi, a_lo, b_hi, b_lo, first, last):
                nc.tensor.matmul(o, a_hi, b_hi, start=first, stop=False)
                nc.tensor.matmul(o, a_hi, b_lo, start=False, stop=False)
                return nc.tensor.matmul(o, a_lo, b_hi, start=False, stop=last)

            def turn_tile(stage, i, src):
                kt, bank = turns[stage][i]
                if stage == 0 and i >= 4:
                    pe.wait_ge(s_tlo, i - 3)
                if stage == 1 and i in (2, 3):
                    pe.wait_ge(s_tlo, KT + i - 1)
                for t in range(NT):
                    mm = nc.tensor.transpose(bank[:, t * P:(t + 1) * P], src[:, t, kt * P:(kt + 1) * P], ident[:, :])
                mm.then_inc(s_tp, 1)

            def columns(bank, k, kt):
                hi, lo = wv_hi(k)[:, kt * P:(kt + 1) * P], wv_lo(k)[:, kt * P:(kt + 1) * P]
                nc.tensor.matmul(bank[:, :], hi, xT_hi[:, kt, :], start=kt == 0, stop=False)
                nc.tensor.matmul(bank[:, :], hi, xT_lo[:, kt, :], start=False, stop=False)
                return nc.tensor.matmul(bank[:, :], lo, xT_hi[:, kt, :], start=False, stop=kt == KT - 1)

            def proj_piece(k, piece):
                kind, a = chunks[k]
                if piece == 0:
                    pe.wait_ge(s_split, release(k) + 1)
                    if 2 <= k < n_proj:
                        pe.wait_ge(s_evac, k - 1)
                if kind == "o":
                    dh, half = a[0], a[1] - 2
                    t, j = 2 * half + piece // 4, piece % 4
                    g = NT * dh + t
                    if j == 0:
                        if g == 0:
                            pe.wait_ge(s_tlo, KT + 4)
                        if g >= 2:
                            pe.wait_ge(s_filled, g - 1)
                    kw, c = k - half + j // 2, (j % 2) * 512
                    mm = three(PROJ[g % 2][:, :], mixT_hi[:, 4 + j, t * P:(t + 1) * P], mixT_lo[:, 4 + j, t * P:(t + 1) * P],
                               wv_hi(kw)[:, c:c + 512], wv_lo(kw)[:, c:c + 512], j == 0, j == 3)
                    if piece == 3:
                        mm.then_inc(s_fill, 1)
                elif kind in ("vg", "dv"):
                    half = a if kind == "vg" else a[1]
                    n = V_COLS if kind == "vg" else 2 * P
                    tt = piece // 4
                    t = 2 * half + tt
                    o = ps[2 + t][:, 0:n] if kind == "vg" else PROJ[k % 2][:, tt * n:(tt + 1) * n]
                    for kt in range(2 * (piece % 4), 2 * (piece % 4) + 2):
                        kw = k - half + kt // 4
                        c = (kt % 4) * n
                        mm = three(o, xT_hi[:, kt, t * P:(t + 1) * P], xT_lo[:, kt, t * P:(t + 1) * P],
                                   wv_hi(kw)[:, c:c + n], wv_lo(kw)[:, c:c + n], kt == 0, kt == KT - 1)
                else:
                    if k == 0:
                        pe.wait_ge(s_tlo, piece + 1)
                    mm = columns(PROJ[k % 2], k, piece)
                if piece == PIECES - 1:
                    mm.then_inc(s_chunk, 1)

            def proj_chunk(k):
                for piece in range(PIECES):
                    proj_piece(k, piece)

            def hidden(kv, j):
                if j == 0:
                    pe.wait_ge(s_evac, kv + 1)
                    pe.wait_ge(s_bvec, 1)
                raw_landed(pe, ("w1", (kv, j)))
                w = raw[:, raw_of[("w1", (kv, j))] % RAW_SLOTS, :]
                for jj in range(4):
                    mm = nc.tensor.matmul(OUTP[kv][0:GROUPS * NC, 0:CMP_HIDDEN],
                                          blk[kv][:, 4 * j + jj, :, :].rearrange("p g n -> p (g n)"),
                                          w[:, jj * CMP_HIDDEN:(jj + 1) * CMP_HIDDEN],
                                          start=(j == 0 and jj == 0), stop=(j == 3 and jj == 3))
                mm.then_inc(s_w1, 1)

            def hidden_turn(kv):
                pe.wait_ge(s_gelu, kv + 1)
                for m in range(2):
                    c = CMP_HIDDEN + m * GROUPS * NC
                    mm = nc.tensor.transpose(OUTP[kv][:, c:c + GROUPS * NC], hid_rows[:, kv, m * P:(m + 1) * P],
                                             ident[0:GROUPS * NC, 0:GROUPS * NC])
                mm.then_inc(s_hid_t, 1)

            def compressed():
                pe.wait_ge(s_small, 16 * 4)
                pe.wait_ge(s_hid_c, 1)
                for m in range(2):
                    mm = nc.tensor.matmul(ps[6][0:HD, 0:GROUPS * NC], w2[:, 0, m, :], hid[:, 0, m, :],
                                          start=m == 0, stop=m == 1)
                mm.then_inc(s_kvc, 1)
                pe.wait_ge(s_hid_c, 2)
                for g in range(GROUPS):
                    for m in range(2):
                        mm = nc.tensor.matmul(ps[7][0:NC, g * HD:(g + 1) * HD], hid[:, 1, m, g * NC:(g + 1) * NC],
                                              w2[:, 1, m, :], start=m == 0, stop=m == 1)
                mm.then_inc(s_kvc, 1)

            def scores(s):
                kind, h, b, i = slots[s]
                bank = SCORE[s % 2]
                pe.wait_ge(s_evac, needed(slots[s]))
                if s >= 2:
                    pe.wait_ge(s_exp, s - 1)
                if kind == "cmp":
                    for hh in range(NSA_HEADS):
                        q = q_nsa[:, hh, i * P:(i + 1) * P]
                        o = bank[:, hh * NC:(hh + 1) * NC]
                        nc.tensor.matmul(o, q, kc_s[:, 0, hh // HEADS_PER_GROUP, :], start=True, stop=False)
                        mm = nc.tensor.matmul(o, q, kc_s[:, 1, hh // HEADS_PER_GROUP, :], start=False, stop=True)
                else:
                    n = (i + 1) * P
                    if kind == "nsa":
                        q = q_nsa[:, h, i * P:(i + 1) * P]
                        k_hi = k_nsa[:, 0, 2 * b + h // HEADS_PER_GROUP, 0:n]
                        k_lo = k_nsa[:, 1, 2 * b + h // HEADS_PER_GROUP, 0:n]
                    else:
                        q = q_diff[:, h % 2, b, i * P:(i + 1) * P]
                        k_hi, k_lo = k_diff[:, h % 2, 0, b, 0:n], k_diff[:, h % 2, 1, b, 0:n]
                    nc.tensor.matmul(bank[:, 0:n], q, k_hi, start=True, stop=False)
                    mm = nc.tensor.matmul(bank[:, 0:n], q, k_lo, start=False, stop=True)
                mm.then_inc(s_qk, 1)

            def turn_probs(s):
                if s not in turn:
                    return
                kind, h, b, i = slots[s]
                n = turn[s]
                if kind == "diff":
                    pe.wait_ge(s_comb, sum(1 for z in turned[:n + 1] if slots[z][0] == "diff"))
                else:
                    pe.wait_ge(s_exp, s + 1)
                if n >= 2:
                    pe.wait_ge(s_pt, n - 1)
                for j in range(2 if kind == "cmp" else i + 1):
                    mm = nc.tensor.transpose(TURN[n % 2][:, j * P:(j + 1) * P], E[:, s % E_SLOTS, j * P:(j + 1) * P],
                                             ident[:, :])
                mm.then_inc(s_turn, 1)

            def values(s):
                if s not in turn:
                    return
                kind, h, b, i = slots[s]
                n = turn[s]
                bank = OUTP[n % 2]
                if n == 0:
                    pe.wait_ge(s_cmp_ready, 1)
                pe.wait_ge(s_pt, n + 1)
                if n >= 2:
                    pe.wait_ge(s_of, n - 1)
                if kind == "cmp":
                    for g in range(GROUPS):
                        mm = nc.tensor.matmul(bank[:, g * 256:(g + 1) * 256], PT[:, n % 2, g * P:(g + 1) * P],
                                              vc_bd[:, g, :], start=True, stop=True)
                else:
                    g = h // HEADS_PER_GROUP
                    for j in range(i + 1):
                        v = v_nsa[:, b, j, g * HD:(g + 1) * HD] if kind == "nsa" else v_diff[:, j, (h % 2) * P:(h % 2 + 1) * P]
                        mm = nc.tensor.matmul(bank[:, 0:v.shape[1]], PT[:, n % 2, j * P:(j + 1) * P], v,
                                              start=j == 0, stop=j == i)
                mm.then_inc(s_pv, 1)

            pe.wait_ge(s_ones, 1)
            for n in range(WARM):
                nc.tensor.matmul(ps[0][:, 0:P], ones[:, :], ones[:, :], start=True, stop=True)
            pe.wait_ge(s_ident, 16)
            pe.wait_ge(s_rows, 16 * 6)
            nc.tensor.transpose(ps[6][:, 0:N_ROWS], rows[0:N_ROWS, :], ident[0:N_ROWS, 0:N_ROWS]).then_inc(s_cols_t, 1)
            pe.wait_ge(s_btab, 16 * 3)
            nc.tensor.matmul(ps[7][0:NHEADS, 0:384], relb[:, :], choice[:, :], start=True, stop=True).then_inc(s_bvec_p, 1)

            pe.wait_ge(s_norm, NT)
            for i in range(KT):
                turn_tile(0, i, mix)
            for k in range(6):
                proj_chunk(k)
                for kv, j in w1_after.get(k, []):
                    hidden(kv, j)
            for piece in range(PIECES):
                if piece == 4:
                    hidden_turn(0)
                proj_piece(6, piece)
            hidden(1, 3)
            upto = 0
            while upto < LEAD_PIECES:
                if upto == 2:
                    hidden_turn(1)
                if upto == 4:
                    compressed()
                proj_piece(n_base + upto // PIECES, upto % PIECES)
                upto += 1
            for s in range(n_slots + 4):
                if 3 <= s < n_slots + 3:
                    turn_probs(s - 3)
                if s < n_slots:
                    scores(s)
                if s >= n_slots:
                    values(s - 4)
                if s == n_slots + 1:
                    pe.wait_ge(s_norm, 2 * NT)
                    for i in (4, 5):
                        turn_tile(1, i, mix)
                if s in (early, early + 1):
                    pe.wait_ge(s_evac, n_proj)
                    pe.wait_ge(s_of, turn[cmp_last] + 1)
                    for i in (2 * (s - early), 2 * (s - early) + 1):
                        turn_tile(1, i, mix)
                while upto < piece_upto[s]:
                    proj_piece(n_base + upto // PIECES, upto % PIECES)
                    upto += 1
                if 4 <= s < n_slots:
                    values(s - 4)

            def rows_chunk(k, a_hi, a_lo, banks, first, last, final=False, filled=False):
                kc = chunks[k][1][1]
                pe.wait_ge(s_split, k + 1)
                order = [(kk, t) for t in range(NT) for kk in range(2)] if final else \
                        [(kk, t) for kk in range(2) for t in (2, 3, 0, 1)]
                for kk, t in order:
                    if filled and kk == 1 and t == 2:
                        pe.wait_ge(s_norm, 3 * NT)
                        for i in (6, 7):
                            turn_tile(1, i, mix)
                    if filled and kk == 0 and t < 2:
                        pe.wait_ge(s_filled, 2 * NT - 1 + t)
                    hi, lo = wv_hi(k)[:, kk * 512:(kk + 1) * 512], wv_lo(k)[:, kk * 512:(kk + 1) * 512]
                    f = 2 * kc + kk
                    mm = three(banks[t][:, :], a_hi[:, f, t * P:(t + 1) * P], a_lo[:, f, t * P:(t + 1) * P],
                               hi, lo, first and kk == 0, last and kk == 1)
                    if final and kk == 1:
                        mm.then_inc(s_last, 1)
                if not final:
                    mm.then_inc(s_chunk, 1)

            pe.wait_ge(s_of, len(turned))
            pe.wait_ge(s_tlo, KT + 6)
            rows_chunk(index[("o", (0, 0))], mixT_hi, mixT_lo, FOUR[0], True, False, filled=True)
            pe.wait_ge(s_tlo, KT + 8)
            rows_chunk(index[("o", (0, 1))], mixT_hi, mixT_lo, FOUR[0], False, True)
            rows_chunk(index[("o", (1, 0))], mixT_hi, mixT_lo, FOUR[1], True, False)
            pe.wait_ge(s_resid, NT)
            for i in range(4):
                turn_tile(2, i, xres)
            rows_chunk(index[("o", (1, 1))], mixT_hi, mixT_lo, FOUR[1], False, True)

            pe.wait_ge(s_tlo, 2 * KT + 4)
            pe.wait_ge(s_split, index[("up", 0)] + 1)
            for kt in range(4):
                columns(PROJ[0], index[("gate", 0)], kt)
            for kt in range(4):
                columns(OUTP[0], index[("up", 0)], kt)
            pe.wait_ge(s_resid, 2 * NT)
            for i in range(4, KT):
                turn_tile(2, i, xres)
            for kind, bank in (("gate", PROJ[0]), ("up", OUTP[0])):
                for kt in range(4, KT):
                    pe.wait_ge(s_tlo, 2 * KT + kt + 1)
                    mm = columns(bank, index[(kind, 0)], kt)
                mm.then_inc(s_chunk, 1)
            for f in range(1, FT):
                for kind, bank, read in (("gate", PROJ[f % 2], s_gn), ("up", OUTP[f % 2], s_un)):
                    k = index[(kind, f)]
                    pe.wait_ge(s_split, k + 1)
                    if f >= 2:
                        pe.wait_ge(read, f - 1)
                    for kt in range(KT):
                        mm = columns(bank, k, kt)
                    mm.then_inc(s_chunk, 1)
                    if k == index[("gate", 1)]:
                        pe.wait_ge(s_diag, 1)
                        nc.tensor.matmul(ps[2][:, :], ones[:, :], diag[:, :], start=True, stop=True).then_inc(s_nb_t, 1)
            for dh in range(2):
                for kc in range(FT // 2):
                    pe.wait_ge(s_alo, 2 * kc + 2 if dh == 0 else FT)
                    rows_chunk(index[("down", (dh, kc))], act_hi, act_lo, FOUR[1 - dh], kc == 0, kc == FT // 2 - 1,
                               final=(dh == 1 and kc == FT // 2 - 1))

        @block.scalar
        def _(act):
            def weights_hi(k):
                if k >= len(chunks):
                    return
                n = chunk_cols(k)
                raw_landed(act, ("chunk", k))
                if k >= SPLIT_SLOTS:
                    act.wait_ge(s_chunk, release(k - SPLIT_SLOTS) + 1)
                nc.scalar.copy(wv_hi(k)[:, 0:n], raw[:, raw_of[("chunk", k)] % RAW_SLOTS, 0:n]).then_inc(s_whi, 1)

            def square(src, junk, col, n):
                if n >= 2:
                    act.wait_ge(s_ss, n - 1)
                nc.scalar.activation(junk, src, ACT.Square, accum_out=stat[:, col:col + 1]).then_inc(s_ss, 1)

            def root(n, *ranges):
                act.wait_ge(s_root_in, n)
                for a, b in ranges:
                    ins = nc.scalar.activation(stat[:, 32 + a:32 + b], stat[:, a:b], ACT.Sqrt)
                ins.then_inc(s_root, 1)

            def split_hi(stage, i, gain):
                kt, bank = turns[stage][i]
                act.wait_ge(s_tp, stage * KT + i + 1)
                nc.scalar.activation((mixT_hi if stage == 1 else xT_hi)[:, kt, :], bank[:, :], ACT.Copy,
                                     scale=cols[:, gain:gain + 1]).then_inc(s_thi, 1)

            def evac_hi(k):
                kind, a = chunks[k]
                if kind not in ("q", "k", "dq", "dk"):
                    return
                act.wait_ge(s_chunk, k + 1)
                if kind in ("dq", "dk") and a >= 2:
                    act.wait_ge(s_qk, last_diff_qk[a - 2] + 1)
                if kind == "dq" and a < 2:
                    act.wait_ge(s_w1, 8)
                for hd in range(2):
                    src = PROJ[k % 2][hd * HD:(hd + 1) * HD, :]
                    if kind in ("q", "dq"):
                        dst = q_nsa[0:HD, 2 * a + hd, :] if kind == "q" else q_diff[0:HD, a % 2, hd, :]
                        ins = nc.scalar.activation(dst, src, ACT.Copy, scale=-SCALE)
                    else:
                        dst = (k_nsa[0:HD, 0, 2 * (a == "kw") + hd, :] if kind == "k"
                               else k_diff[0:HD, a % 2, 0, hd, :])
                        ins = nc.scalar.activation(dst, src, ACT.Copy)
                    ins.then_inc(s_hi, 1)

            def gelu(kv):
                act.wait_ge(s_w1, w1_order.index((kv, 3)) + 1)
                nc.scalar.activation(hid_rows[:, kv, :], OUTP[kv][0:GROUPS * NC, 0:CMP_HIDDEN],
                                     ACT.Gelu_apprx_tanh).then_inc(s_gelu, 1)

            def load_bias(n):
                h = bias_order[n]
                if n == 0:
                    act.wait_ge(s_spread, 16)
                if n >= BIAS_SLOTS:
                    act.wait_ge(s_add, bias_last[bias_order[n - BIAS_SLOTS]] + 1)
                base = bias_rows[h, 0, :]
                src = bass.AP(base.tensor, base.offset + 127, [[383, P], [1, 256]])
                act.dma_start(bias[:, n % BIAS_SLOTS, 256:512], src).then_inc(s_bias[n % BIAS_SLOTS], 16)

            def exps(s):
                kind, h, b, i = slots[s]
                n = 256 if kind == "cmp" else (i + 1) * P
                act.wait_ge(s_add, s + 1)
                if s >= E_SLOTS:
                    last = s - E_SLOTS
                    if last not in turn:
                        last += 1
                    act.wait_ge(s_turn, turns_upto[last])
                if kind == "cmp":
                    nc.scalar.activation(E[:, s % E_SLOTS, 0:n], SCORE[s % 2][:, 0:n], ACT.Exp, scale=-1.0).then_inc(s_exp, 1)
                else:
                    nc.scalar.activation(E[:, s % E_SLOTS, 0:n], SCORE[s % 2][:, 0:n], ACT.Exp, scale=-1.0,
                                         bias=nmax[:, s:s + 1], accum_out=ssum[:, s:s + 1]).then_inc(s_exp, 1)

            def copy_turned(s):
                if s not in turn:
                    return
                kind, h, b, i = slots[s]
                n = turn[s]
                w = 256 if kind == "cmp" else (i + 1) * P
                act.wait_ge(s_turn, n + 1)
                if n >= 2:
                    act.wait_ge(s_pv, n - 1)
                nc.scalar.copy(PT[:, n % 2, 0:w], TURN[n % 2][:, 0:w]).then_inc(s_pt, 1)

            def free_weights(s):
                for k in chunks_done_in[s]:
                    for j in (k - 1, k):
                        if release(j) == k:
                            weights_hi(j + SPLIT_SLOTS)

            act.wait_ge(s_zero, 1)
            nc.scalar.activation(stat[:, 63:64], stat[:, 62:63], ACT.Sqrt)
            for t in range(NT):
                if t % 2 == 0:
                    act.wait_ge(s_x[t], 16)
                    square(xres[:, t, :], E[:, t:t + 2, :].rearrange("p a b -> p (a b)"), 20 + t, t // 2)
                root(t + 1, (20 + t, 21 + t))
                if t == 2:
                    weights_hi(0)
            weights_hi(1)
            act.wait_ge(s_cols, 1)
            for i in range(KT):
                split_hi(0, i, C_N1 + i)
            weights_hi(2)
            act.wait_ge(s_bvec, 1)
            act.dma_start(bias_scratch[:, :], bias_vec[:, :]).then_inc(s_scratch, 16)
            act.wait_ge(s_lamdot, 1)
            nc.scalar.activation(lam[:, 2:4], lam[:, 0:2], ACT.Exp).then_inc(s_lamexp, 1)
            weights_hi(3)
            weights_hi(4)
            evac_hi(2)
            weights_hi(5)
            act.wait_ge(s_scratch, 16)
            act.dma_start(bias_rows[:, :, :], bias_scratch[:, :].unsqueeze(1).to_broadcast([NHEADS, P, 384])).then_inc(s_spread, 16)
            act.wait_ge(s_evac, 5)
            nc.scalar.activation(gates[:, :, :], gates[:, :, :], ACT.Exp, scale=-1.0).then_inc(s_gexp, 1)
            load_bias(0)
            load_bias(1)
            weights_hi(6)
            evac_hi(5)
            gelu(0)
            weights_hi(7)
            weights_hi(8)
            evac_hi(6)
            gelu(1)
            weights_hi(9)
            weights_hi(10)
            act.wait_ge(s_kvc, 1)
            nc.scalar.copy(kc_s[0:HD, 0, :, :].rearrange("p g n -> p (g n)"), ps[6][0:HD, 0:GROUPS * NC]).then_inc(s_kchi, 1)

            for s in range(n_slots + 4):
                if 3 <= s < n_slots + 3:
                    copy_turned(s - 3)
                if s < n_slots:
                    for n in range(2, NHEADS):
                        if s == bias_first[bias_order[n - 1]]:
                            load_bias(n)
                    exps(s)
                    for k in chunks_done_in[s]:
                        evac_hi(k)
                    free_weights(s)
                else:
                    if s == n_slots + 1:
                        for i in (4, 5):
                            split_hi(1, i, C_SUB)
                    if s == n_slots + 3:
                        root(6, (8, 16))
                    free_weights(s)
                if s in (early, early + 1):
                    for i in (2 * (s - early), 2 * (s - early) + 1):
                        split_hi(1, i, C_NSA + i)
                if s - 5 in cmp_slot:
                    t = cmp_slot.index(s - 5)
                    act.wait_ge(s_of, turn[s - 5] + 1)
                    square(mix[:, t, 512:1024], mixT_lo[:, t, :], 16 + t, 2 + t)
                if s == early + 1:
                    root(5, (0, 8), (16, 20))
                if s == n_slots:
                    act.wait_ge(s_zero, 1)
                    nc.scalar.activation(stat[:, 63:64], stat[:, 62:63], ACT.Sqrt)

            for i in range(6, KT):
                split_hi(1, i, C_SUB)
            for n in range(2):
                weights_hi(n_fill + n + SPLIT_SLOTS)
            for t in range(NT):
                act.wait_ge(s_resid, t + 1)
                square(xres[:, t, 0:512], E[:, t % 2, :], 20 + t, 6 + t)
            weights_hi(n_fill + 2 + SPLIT_SLOTS)
            for i in range(4):
                split_hi(2, i, C_N2 + i)
            weights_hi(n_fill + 3 + SPLIT_SLOTS)
            for i in range(4, KT):
                split_hi(2, i, C_N2 + i)
            for t in range(NT):
                act.wait_ge(s_resid, NT + t + 1)
                square(xres[:, t, 512:1024], E[:, t % 2, :], 24 + t, 10 + t)
            root(7, (20, 24))
            act.wait_ge(s_nb_t, 1)
            nc.scalar.copy(norm_b[:, :], ps[2][:, :]).then_inc(s_nb, 1)
            act.dma_start(final_g[:, :], final_norm.partition_broadcast(P)).then_inc(s_final_g, 16)
            for f in range(FT):
                weights_hi(index[("gate", f)] + SPLIT_SLOTS)
                act.wait_ge(s_gn, f + 1)
                nc.scalar.activation(gate_n[:, f % 2, :], gate_n[:, f % 2, :], ACT.Silu).then_inc(s_silu, 1)
                weights_hi(index[("up", f)] + SPLIT_SLOTS)
                act.wait_ge(s_prod, f + 1)
                nc.scalar.copy(act_hi[:, f, :], up_n[:, f % 2, :]).then_inc(s_ahi, 1)
            for kc in range(FT // 2):
                weights_hi(index[("down", (0, kc))] + SPLIT_SLOTS)
            for t in range(NT):
                act.wait_ge(s_resid, 2 * NT + t + 1)
                square(xres[:, t, 0:512], gate_n[:, t % 2, :], 20 + t, 14 + t)
            nc.scalar.activation(stat[:, 63:64], stat[:, 62:63], ACT.Sqrt)
            for kc in range(FT // 2 - SPLIT_SLOTS):
                weights_hi(index[("down", (1, kc))] + SPLIT_SLOTS)
            for t in range(NT):
                act.wait_ge(s_resid, 3 * NT + t + 1)
                square(xres[:, t, 512:1024], gate_n[:, t % 2, :], 24 + t, 18 + t)
                if t == 1:
                    root(8, (20, 21))
                if t == 2:
                    root(9, (21, 22))
            root(10, (22, 24))
            act.wait_ge(s_final, 3)
            nc.scalar.activation(xres[:, NT - 1, 0:512], xres[:, NT - 1, 0:512], ACT.Copy,
                                 scale=stat[:, 52 + NT - 1:52 + NT]).then_inc(s_ya, 1)

        @block.vector
        def _(dve):
            chain = [0]

            def link(ins):
                chain[0] += 1
                ins.then_inc(s_dve, 1)
                dve.wait_ge(s_dve, chain[0])

            def mean_root(*ranges):
                for a, b, width in ranges:
                    ins = nc.vector.tensor_scalar(stat[:, a:b], stat[:, a:b], 1.0 / width, EPS, ALU.mult, ALU.add)
                ins.then_inc(s_root_in, 1)

            def inverse_root(n, *ranges):
                dve.wait_ge(s_root, n)
                for a, b in ranges:
                    ins = nc.vector.reciprocal(stat[:, 32 + a:32 + b], stat[:, 32 + a:32 + b])
                link(ins)

            def scale_diff(t, pair):
                m = mix[:, t, 2 * P * pair:2 * P * (pair + 1)].rearrange("p (h n) -> p h n", n=P)
                c = 32 + 8 * pair + t
                r = stat[:, c:c + 5:4]
                return nc.vector.tensor_tensor(m, m, r.unsqueeze(2).to_broadcast([P, 2, P]), ALU.mult)

            def split_lo(stage, i, gain):
                kt, bank = turns[stage][i]
                hi, lo = (mixT_hi, mixT_lo) if stage == 1 else (xT_hi, xT_lo)
                dve.wait_ge(s_thi, stage * KT + i + 1)
                nc.vector.scalar_tensor_tensor(out=lo[:, kt, :], in0=bank[:, :], scalar=cols[:, gain:gain + 1],
                                               in1=hi[:, kt, :].bitcast(F32),
                                               op0=ALU.mult, op1=ALU.subtract).then_inc(s_tlo, 1)

            def evac(k):
                kind, a = chunks[k]
                bank = PROJ[k % 2]
                dve.wait_ge(s_chunk, k + 1)
                if kind == "c":
                    for par in range(2):
                        for g in range(GROUPS):
                            src = bank[g * HD:(g + 1) * HD, :]
                            src = bass.AP(src.tensor, src.offset + par, [src.ap[0], [2, 16], [CMP_STRIDE, N_CMP]])
                            pos = cols[par * HD:(par + 1) * HD, C_POS + 16 * a:C_POS + 16 * a + 16]
                            ins = nc.vector.tensor_tensor(blk[a][par * HD:(par + 1) * HD, :, g, 0:N_CMP], src,
                                                          pos.unsqueeze(2).to_broadcast([HD, 16, N_CMP]), ALU.add)
                elif kind == "vg":
                    for t in (2 * a, 2 * a + 1):
                        nc.vector.tensor_copy(gates[:, t, :], ps[2 + t][:, 2 * P:V_COLS])
                        ins = nc.vector.tensor_copy(v_nsa[:, :, t, :], ps[2 + t][:, 0:2 * P].rearrange("p (b n) -> p b n", b=2))
                elif kind == "dv":
                    pair, half = a
                    if pair == 1:
                        dve.wait_ge(s_pv, turn[last_diff_qk[1]] + 1)
                    ins = nc.vector.tensor_copy(v_diff[:, 2 * half:2 * half + 2, :].rearrange("p t n -> p (t n)"), bank[:, :])
                else:
                    for hd in range(2):
                        src = bank[hd * HD:(hd + 1) * HD, :]
                        dve.wait_ge(s_hi, hi_upto[k] - 1 + hd)
                        if kind in ("q", "dq"):
                            q = q_nsa[:, 2 * a + hd, :] if kind == "q" else q_diff[:, a % 2, hd, :]
                            ins = nc.vector.scalar_tensor_tensor(out=q[HD:P, :], in0=src, scalar=-SCALE,
                                                                 in1=q[0:HD, :].bitcast(F32),
                                                                 op0=ALU.mult, op1=ALU.subtract)
                        else:
                            if kind == "k":
                                hi, lo = (k_nsa[:, z, 2 * (a == "kw") + hd, :] for z in range(2))
                            else:
                                hi, lo = (k_diff[:, a % 2, z, hd, :] for z in range(2))
                            link(nc.vector.tensor_tensor(lo[0:HD, :], src, hi[0:HD, :].bitcast(F32), ALU.subtract))
                            nc.vector.tensor_copy(hi[HD:P, :], hi[0:HD, :])
                            ins = nc.vector.tensor_copy(lo[HD:P, :], lo[0:HD, :])
                ins.then_inc(s_evac, 1)

            def add_bias(s):
                kind, h, b, i = slots[s]
                bank = SCORE[s % 2]
                dve.wait_ge(s_qk, s + 1)
                if kind == "cmp":
                    z = bank[:, 0:NSA_HEADS * NC].rearrange("p (h n) -> p h n", n=NC)
                    link(nc.vector.tensor_tensor(z, z, cmask[:, i, :].unsqueeze(1).to_broadcast([P, NSA_HEADS, NC]), ALU.add))
                    link(nc.vector.tensor_reduce(cstat[:, i, 0, :], z, AX.X, ALU.min))
                    nc.vector.tensor_tensor(z, z, cstat[:, i, 0, :].unsqueeze(2).to_broadcast([P, NSA_HEADS, NC]),
                                            ALU.subtract).then_inc(s_add, 1)
                    return
                n = (i + 1) * P
                m = bias_order.index(bias_head(slots[s]))
                dve.wait_ge(s_bias[m % BIAS_SLOTS], 16 * (m // BIAS_SLOTS + 1))
                nc.vector.tensor_tensor_reduce(out=bank[:, 0:n], in0=bank[:, 0:n],
                                               in1=bias[:, m % BIAS_SLOTS, 512 - n:512], scale=1.0, scalar=3.0e38,
                                               op0=ALU.add, op1=ALU.min, accum_out=nmax[:, s:s + 1]).then_inc(s_add, 1)

            def weigh(s):
                kind, h, b, i = slots[s]
                dve.wait_ge(s_exp, s + 1)
                if kind == "cmp":
                    z = E[:, s % E_SLOTS, 0:256].rearrange("p (h n) -> p h n", n=NC)
                    link(nc.vector.tensor_reduce(cstat[:, i, 1, :], z, AX.X, ALU.add))
                    link(nc.vector.reciprocal(cstat[:, i, 2, :], cstat[:, i, 1, :]))
                    g0 = gates[:, i, :].rearrange("p (h c) -> p h c", c=3)[:, :, 0]
                    link(nc.vector.scalar_tensor_tensor(out=cstat[:, i, 3, :], in0=g0, scalar=has_cmp[:, i:i + 1],
                                                        in1=cstat[:, i, 2, :], op0=ALU.mult, op1=ALU.mult))
                    return
                if kind == "diff" and b == 0:
                    return
                link(nc.vector.reciprocal(ssum[:, s:s + 1], ssum[:, s:s + 1]))
                if kind == "nsa":
                    c = 3 * h + 1 + b
                    nc.vector.tensor_tensor(coef[:, s:s + 1], ssum[:, s:s + 1], gates[:, i, c:c + 1], ALU.mult).then_inc(s_coefs, 1)
                elif b == 1:
                    n = (i + 1) * P
                    e0, e1 = E[:, (s - 1) % E_SLOTS, 0:n], E[:, s % E_SLOTS, 0:n]
                    link(nc.vector.scalar_tensor_tensor(out=coef[:, s:s + 1], in0=ssum[:, s - 1:s], scalar=lam[:, 6:7],
                                                        in1=ssum[:, s:s + 1], op0=ALU.mult, op1=ALU.mult))
                    nc.vector.scalar_tensor_tensor(out=e1, in0=e1, scalar=coef[:, s:s + 1], in1=e0,
                                                   op0=ALU.mult, op1=ALU.add).then_inc(s_comb, 1)
                    link(nc.vector.reciprocal(coef[:, s - 1:s], ssum[:, s - 1:s]))

            def gather(s):
                if s not in turn:
                    return
                kind, h, b, i = slots[s]
                n = turn[s]
                bank = OUTP[n % 2]
                dve.wait_ge(s_pv, n + 1)
                if kind == "nsa":
                    dve.wait_ge(s_coefs, sum(1 for z in turned[:n + 1] if slots[z][0] == "nsa"))
                    m = mix[:, i, 512 + h * HD:512 + (h + 1) * HD]
                    if b == 0:
                        nc.vector.tensor_scalar(m, bank[:, 0:HD], coef[:, s:s + 1], None, ALU.mult).then_inc(s_of, 1)
                    else:
                        dve.wait_ge(s_of, n)
                        nc.vector.scalar_tensor_tensor(out=m, in0=bank[:, 0:HD], scalar=coef[:, s:s + 1], in1=m,
                                                       op0=ALU.mult, op1=ALU.add).then_inc(s_of, 1)
                elif kind == "diff":
                    m = mix[:, i, h * P:(h + 1) * P]
                    nc.vector.tensor_scalar(m, bank[:, 0:P], coef[:, s - 1:s], None, ALU.mult).then_inc(s_of, 1)
                    dve.wait_ge(s_of, n + 1)
                    c = 4 * h + i
                    link(nc.vector.tensor_tensor_reduce(out=sq[:, 0:P], in0=m, in1=m, scale=1.0, scalar=0.0, op0=ALU.mult,
                                                        op1=ALU.add, accum_out=stat[:, c:c + 1]))
                else:
                    z = bank[:, :].rearrange("p (h n) -> p h n", n=HD)
                    link(nc.vector.tensor_tensor(sq[:, :].rearrange("p (h n) -> p h n", n=HD), z,
                                                 cstat[:, i, 3, :].unsqueeze(2).to_broadcast([P, NSA_HEADS, HD]), ALU.mult))
                    m = mix[:, i, 512:1024]
                    nc.vector.tensor_tensor(m, m, sq[:, :], ALU.add).then_inc(s_of, 1)
                    dve.wait_ge(s_of, n + 1)

            def add_group(g):
                dh, t = g // NT, g % NT
                if g % 2 == 0:
                    dve.wait_ge(s_fill, g // 2 + 1)
                else:
                    dve.wait_ge(s_chunk, n_proj + g // 2 + 1)
                z = xres[:, t, dh * 512:(dh + 1) * 512]
                nc.vector.scalar_tensor_tensor(out=z, in0=PROJ[g % 2][:, :], scalar=stat[:, 48 + t:49 + t], in1=z,
                                               op0=ALU.mult, op1=ALU.add).then_inc(s_filled, 1)

            nc.vector.memset(stat[:, 60:64], 1.0).then_inc(s_zero, 1)
            nc.vector.memset(ones[:, :], 1.0).then_inc(s_ones, 1)
            nc.vector.memset(bias[:, :, 0:256], 0.0)
            nc.vector.memset(vc_bd[:, :, :], 0.0)
            for kv in range(2):
                nc.vector.memset(blk[kv][:, :, :, N_CMP:NC], 0.0)
            link(nc.vector.memset(sq[:, :], 0.0))
            for t in range(NT):
                if t % 2 == 0:
                    dve.wait_ge(s_ss, t // 2 + 1)
                else:
                    dve.wait_ge(s_x[t], 16)
                    link(nc.vector.tensor_tensor_reduce(out=mix[:, t, :], in0=xres[:, t, :], in1=xres[:, t, :], scale=1.0,
                                                        scalar=0.0, op0=ALU.mult, op1=ALU.add,
                                                        accum_out=stat[:, 20 + t:21 + t]))
                mean_root((20 + t, 21 + t, D))
                inverse_root(t + 1, (20 + t, 21 + t))
                nc.vector.tensor_scalar(mix[:, t, :], xres[:, t, :], stat[:, 52 + t:53 + t], None, ALU.mult).then_inc(s_norm, 1)
            dve.wait_ge(s_cols_t, 1)
            link(nc.vector.tensor_copy(cols[:, 0:N_ROWS], ps[6][:, 0:N_ROWS]))
            nc.vector.tensor_scalar(cols[:, C_SUB:C_SUB + 1], cols[:, C_SUB:C_SUB + 1], 1.0 - LAMBDA_INIT, None,
                                    ALU.mult).then_inc(s_cols, 1)
            dve.wait_ge(s_bvec_p, 1)
            nc.vector.tensor_tensor(bias_vec[:, :], ps[7][0:NHEADS, 0:384], causal[:, :], ALU.add).then_inc(s_bvec, 1)
            dve.wait_ge(s_cols, 1)
            for i in range(KT):
                split_lo(0, i, C_N1 + i)
            dve.wait_ge(s_lamin, 16 * 4)
            for n in range(2):
                ins = nc.vector.tensor_tensor_reduce(out=sq[:, n * HD:(n + 1) * HD], in0=lam_in[:, 2 * n, :],
                                                     in1=lam_in[:, 2 * n + 1, :], scale=1.0, scalar=0.0, op0=ALU.mult,
                                                     op1=ALU.add, accum_out=lam[:, n:n + 1])
            ins.then_inc(s_lamdot, 1)
            dve.wait_ge(s_lamexp, 1)
            link(nc.vector.tensor_tensor(lam[:, 5:6], lam[:, 3:4], lam[:, 2:3], ALU.subtract))
            link(nc.vector.tensor_scalar(lam[:, 6:7], lam[:, 5:6], -LAMBDA_INIT, None, ALU.add))
            for k in range(5):
                evac(k)
            dve.wait_ge(s_gexp, 1)
            link(nc.vector.tensor_scalar(gates[:, :, :], gates[:, :, :], 1.0, None, ALU.add))
            link(nc.vector.reciprocal(gates[:, :, :], gates[:, :, :]))
            evac(5)
            for kv in range(2):
                if kv == 1:
                    evac(6)
                dve.wait_ge(s_hid_t, kv + 1)
                nc.vector.tensor_copy(hid[:, kv, :, :].rearrange("p m n -> p (m n)"),
                                      OUTP[kv][:, CMP_HIDDEN:CMP_HIDDEN + 2 * GROUPS * NC]).then_inc(s_hid_c, 1)
            dve.wait_ge(s_kchi, 1)
            k_hi, k_lo = (kc_s[:, z, :, :].rearrange("p g n -> p (g n)") for z in range(2))
            link(nc.vector.tensor_tensor(k_lo[0:HD, :], ps[6][0:HD, 0:GROUPS * NC], k_hi[0:HD, :].bitcast(F32), ALU.subtract))
            nc.vector.tensor_copy(k_hi[HD:P, :], k_hi[0:HD, :])
            nc.vector.tensor_copy(k_lo[HD:P, :], k_lo[0:HD, :])
            dve.wait_ge(s_kvc, 2)
            for g in range(GROUPS):
                for hh in range(HEADS_PER_GROUP):
                    ins = nc.vector.tensor_copy(vc_bd[hh * NC:(hh + 1) * NC, g, hh * HD:(hh + 1) * HD],
                                                ps[7][0:NC, g * HD:(g + 1) * HD])
            ins.then_inc(s_cmp_ready, 1)

            for s in range(n_slots + 4):
                if s < n_slots:
                    add_bias(s)
                if 1 <= s < n_slots + 1:
                    weigh(s - 1)
                if s >= 4:
                    gather(s - 4)
                if s < n_slots:
                    for k in chunks_done_in[s]:
                        if k < n_proj:
                            evac(k)
                if s in (early, early + 1):
                    for i in (2 * (s - early), 2 * (s - early) + 1):
                        split_lo(1, i, C_NSA + i)
                if s == early:
                    dve.wait_ge(s_ss, 6)
                    mean_root((0, 8, P), (16, 20, 512))
                if s == early + 2:
                    inverse_root(5, (0, 8), (16, 20))
                if early + 3 <= s < early + 3 + NT:
                    scale_diff(s - early - 3, 0).then_inc(s_norm, 1)
                if s == n_slots + 1:
                    for i in (4, 5):
                        split_lo(1, i, C_SUB)
                if s < n_slots + 3:
                    for g in groups_done_in[s]:
                        add_group(g)

            mean_root((8, 16, P))
            last_groups = groups_done_in[n_slots + 3]
            for g in last_groups[:1]:
                add_group(g)
            inverse_root(6, (8, 16))
            for t in range(NT):
                scale_diff(t, 1).then_inc(s_norm, 1)
            for g in last_groups[1:]:
                add_group(g)
            for i in range(6, KT):
                split_lo(1, i, C_SUB)

            def add_residual(t, dh, banks):
                z = xres[:, t, dh * 512:(dh + 1) * 512]
                nc.vector.tensor_tensor(z, z, banks[t][:, :], ALU.add).then_inc(s_resid, 1)

            def sum_halves():
                link(nc.vector.tensor_tensor(stat[:, 20:24], stat[:, 20:24], stat[:, 24:28], ALU.add))

            dve.wait_ge(s_filled, 2 * NT)
            for dh in range(2):
                dve.wait_ge(s_chunk, index[("o", (dh, 1))] + 1)
                for t in range(NT):
                    add_residual(t, dh, FOUR[dh])
                for i in range(4 * dh, 4 * dh + 4):
                    split_lo(2, i, C_N2 + i)
            dve.wait_ge(s_ss, 14)
            sum_halves()
            mean_root((20, 24, D))
            inverse_root(7, (20, 24))
            for t in range(NT):
                ins = nc.vector.tensor_scalar(diag[:, t * P:(t + 1) * P], ident[:, :], stat[:, 52 + t:53 + t], None, ALU.mult)
            ins.then_inc(s_diag, 1)
            dve.wait_ge(s_nb, 1)
            for f in range(FT):
                dve.wait_ge(s_chunk, index[("gate", f)] + 1)
                if f >= 2:
                    dve.wait_ge(s_prod, f - 1)
                nc.vector.tensor_tensor(gate_n[:, f % 2, :], PROJ[f % 2][:, :], norm_b[:, :], ALU.mult).then_inc(s_gn, 1)
                dve.wait_ge(s_chunk, index[("up", f)] + 1)
                if f >= 2:
                    dve.wait_ge(s_alo, f - 1)
                    dve.wait_ge(s_ahi, f - 1)
                nc.vector.tensor_tensor(up_n[:, f % 2, :], OUTP[f % 2][:, :], norm_b[:, :], ALU.mult).then_inc(s_un, 1)
                dve.wait_ge(s_un, f + 1)
                dve.wait_ge(s_silu, f + 1)
                nc.vector.tensor_tensor(up_n[:, f % 2, :], gate_n[:, f % 2, :], up_n[:, f % 2, :], ALU.mult).then_inc(s_prod, 1)
                dve.wait_ge(s_ahi, f + 1)
                nc.vector.tensor_tensor(act_lo[:, f, :], up_n[:, f % 2, :], act_hi[:, f, :].bitcast(F32),
                                        ALU.subtract).then_inc(s_alo, 1)
            dve.wait_ge(s_chunk, index[("down", (0, FT // 2 - 1))] + 1)
            for t in range(NT):
                add_residual(t, 0, FOUR[1])
            dve.wait_ge(s_final_g, 16)
            for t in range(NT):
                dve.wait_ge(s_ss, 14 + t + 1)
                z = xres[:, t, 0:512]
                ins = nc.vector.tensor_tensor(z, z, final_g[:, 0:512], ALU.mult)
            link(ins)
            link(nc.vector.tensor_scalar(stat[:, 20:24], stat[:, 20:24], 1.0 / D, EPS, ALU.mult, ALU.add))

            def final_mean(a, b):
                dve.wait_ge(s_ss, 18 + b)
                nc.vector.scalar_tensor_tensor(out=stat[:, 20 + a:20 + b], in0=stat[:, 24 + a:24 + b], scalar=1.0 / D,
                                               in1=stat[:, 20 + a:20 + b], op0=ALU.mult, op1=ALU.add).then_inc(s_root_in, 1)

            def final_inverse(n, a, b):
                dve.wait_ge(s_root, 7 + n)
                nc.vector.reciprocal(stat[:, 52 + a:52 + b], stat[:, 52 + a:52 + b]).then_inc(s_final, 1)
                dve.wait_ge(s_final, n)

            def final_scale(t):
                dve.wait_ge(s_gx, t + 1)
                nc.vector.tensor_scalar(xres[:, t, :], xres[:, t, :], stat[:, 52 + t:53 + t], None, ALU.mult).then_inc(s_y, 1)

            for t in range(NT):
                dve.wait_ge(s_last, t + 1)
                add_residual(t, 1, FOUR[0])
                if t == 1:
                    final_mean(0, 1)
                if t == 2:
                    final_mean(1, 2)
                    final_inverse(1, 0, 1)
                    final_scale(0)
            final_inverse(2, 1, 2)
            final_scale(1)
            final_mean(2, NT)
            final_inverse(3, 2, NT)
            z = xres[:, NT - 1, 512:1024]
            nc.vector.scalar_tensor_tensor(out=z, in0=z, scalar=stat[:, 52 + NT - 1:52 + NT], in1=final_g[:, 512:1024],
                                           op0=ALU.mult, op1=ALU.mult).then_inc(s_y, 1)
            final_scale(2)


_INS = ["x", "norm1", "w_in", "lambda_q1", "lambda_k1", "lambda_q2", "lambda_k2", "diff_subln",
        "cmp_pos_k", "cmp_w1_k", "cmp_w2_k", "cmp_pos_v", "cmp_w1_v", "cmp_w2_v", "nsa_norm",
        "w_out", "norm2", "w_gate", "w_up", "w_down", "rel_bias", "final_norm"]


def kernel(**inputs):
    import concourse.bacc as _bacc
    from concourse.bass_utils import run_bass_kernel_spmd as _run

    nc = _bacc.Bacc("TRN2", target_bir_lowering=False, num_devices=1)
    arrays, args = {}, []
    for name in _INS:
        arrays[f"in_{name}_dram"] = np.ascontiguousarray(inputs[name])
    for name, a in shape_constants().items():
        arrays[f"in_{name}_dram"] = np.ascontiguousarray(a)
    for name, a in arrays.items():
        args.append(nc.dram_tensor(name, a.shape, mybir.dt.from_np(a.dtype), kind="ExternalInput").ap())
    args.append(nc.dram_tensor("bias_scratch", (NHEADS, 384), F32).ap())
    args.append(nc.dram_tensor("bias_rows", (NHEADS, P, 384), F32).ap())
    args.append(nc.dram_tensor("out_0_dram", (1, T, D), F32, kind="ExternalOutput").ap())
    hymba_block(nc, *args)
    r = _run(nc, [arrays], core_ids=[0])
    return r.results[0]["out_0_dram"]
```
